# Optimizing a Trainium2 kernel written in Bass

```python
import jax, jax.numpy as jnp
from jax import lax
import numpy as np

D_MODEL = 1024
BATCH = 1
SEQ = 2048
DEPTH = 1
DEC_BATCH = 8
DEC_SEQ = 8
PAST_LEN = 16384
PAGE_SIZE = 128

HEAD_DIM = 64
D_RWKV = 768
N_HEADS = D_RWKV // HEAD_DIM
D_POOL = 256
POOL_WINDOWS = (2, 4, 8, 16)
N_POOL_GROUPS = len(POOL_WINDOWS)
POOL_GROUP_DIM = D_POOL // N_POOL_GROUPS
POOL_BUF = max(POOL_WINDOWS) - 1
LORA_DECAY = 64
LORA_ICLR = 64
LORA_VRES = 32
LORA_GATE = 128
D_SHIFT = 3 * D_RWKV + LORA_DECAY + LORA_ICLR + LORA_GATE
D_GATES = 2 * D_MODEL
D_IN = D_SHIFT + D_POOL + D_GATES
D_FF = -(-8 * D_MODEL // (3 * 256)) * 256
RMS_EPS = 1e-6
GN_EPS = 1e-5 * HEAD_DIM

kernel_name = 'rwkv7_pool_gated_hybrid_step'

def _rmsnorm(x, g):
    xf = x.astype(jnp.float32)
    y = xf * lax.rsqrt(jnp.mean(xf * xf, axis=-1, keepdims=True) + RMS_EPS)
    return (y * g.astype(jnp.float32)).astype(x.dtype)

def _wkv_recurrence(s0, r, w, k, v, kk, a):
    def step(s, inp):
        r_t, w_t, k_t, v_t, kk_t, a_t = inp
        sa = jnp.einsum('bhvk,bhk->bhv', s, -kk_t)
        s = (s * w_t[:, :, None, :]
             + sa[..., None] * (kk_t * a_t)[:, :, None, :]
             + v_t[..., None] * k_t[:, :, None, :])
        return s, jnp.einsum('bhvk,bhk->bhv', s, r_t)
    xs = tuple(jnp.swapaxes(z, 0, 1) for z in (r, w, k, v, kk, a))
    s_final, o = lax.scan(step, s0, xs)
    return s_final, jnp.swapaxes(o, 0, 1)

def _pool_mixer(u, buf, start_pos, pool_map, pool_scale):
    b, t, _ = u.shape
    uf = u.astype(jnp.float32)
    full = jnp.concatenate([buf.astype(jnp.float32), uf], axis=1)
    csum = jnp.concatenate([jnp.zeros_like(full[:, :1]), jnp.cumsum(full, axis=1)], axis=1)
    upto = csum[:, POOL_BUF + 1:]
    pos = start_pos + jnp.arange(t, dtype=jnp.int32)
    means = []
    for gi, win in enumerate(POOL_WINDOWS):
        c0 = gi * POOL_GROUP_DIM
        c1 = c0 + POOL_GROUP_DIM
        before = csum[:, POOL_BUF + 1 - win:POOL_BUF + 1 - win + t, c0:c1]
        count = jnp.minimum(pos + 1, win).astype(jnp.float32)[None, :, None]
        means.append((upto[..., c0:c1] - before) / count)
    diff = (jnp.concatenate(means, axis=-1) - uf).reshape(b, t, N_POOL_GROUPS, POOL_GROUP_DIM)
    out = jnp.einsum('btgc,gcd->btgd', diff, pool_map.astype(jnp.float32)).reshape(b, t, D_POOL)
    out = out * pool_scale.astype(jnp.float32)
    return out, full[:, -POOL_BUF:].astype(buf.dtype)

def _block(x, shift_prev, wkv_prev, pool_prev, start_pos, v_first, vres, lw):
    (g_mix_pre, g_mix_post, g_ffn_pre, g_ffn_post, w_in, mu_shift, decay_bias, w_decay_up,
     iclr_bias, w_iclr_up, w_gate_up, k_k, k_a, r_k, ln_x_w, ln_x_b, pool_map, pool_scale,
     w_branch_rwkv, w_branch_pool, w_out, w_ffn_in, w_ffn_out) = lw
    f32 = jnp.float32
    b, t, _ = x.shape
    xn = _rmsnorm(x, g_mix_pre)
    proj = jnp.einsum('btd,de->bte', xn, w_in)
    ps = proj[..., :D_SHIFT]
    ps_prev = jnp.concatenate([shift_prev[:, None, :].astype(ps.dtype), ps[:, :-1]], axis=1)
    mixed = (ps + (ps_prev - ps) * mu_shift).astype(f32)
    o1, o2, o3 = D_RWKV, 2 * D_RWKV, 3 * D_RWKV
    o4 = o3 + LORA_DECAY
    o5 = o4 + LORA_ICLR
    r, k, v = mixed[..., :o1], mixed[..., o1:o2], mixed[..., o2:o3]
    xw, xa, xg = mixed[..., o3:o4], mixed[..., o4:o5], mixed[..., o5:]
    u = proj[..., D_SHIFT:D_SHIFT + D_POOL]
    gate_rwkv, gate_pool = jnp.split(jax.nn.sigmoid(proj[..., D_SHIFT + D_POOL:]), 2, axis=-1)

    log_w = -jax.nn.softplus(-(decay_bias + jnp.tanh(xw) @ w_decay_up)) - 0.5
    decay = jnp.exp(-jnp.exp(log_w))
    a = jax.nn.sigmoid(iclr_bias + xa @ w_iclr_up)
    g = jax.nn.sigmoid(xg) @ w_gate_up
    if vres is None:
        v_first = v
    else:
        vres_bias, w_vres_down, w_vres_up = vres
        v = v + (v_first - v) * jax.nn.sigmoid(vres_bias + (xn @ w_vres_down) @ w_vres_up)
    heads = lambda z: z.reshape(b, t, N_HEADS, HEAD_DIM)
    kk = heads(k * k_k)
    kk = kk / jnp.maximum(jnp.sqrt(jnp.sum(kk * kk, axis=-1, keepdims=True)), 1e-12)
    k = k * (1.0 + (a - 1.0) * k_a)
    rh, kh, vh, ah, wh = heads(r), heads(k), heads(v), heads(a), heads(decay)
    s_new, o = _wkv_recurrence(wkv_prev.astype(f32), rh, wh, kh, vh, kk, ah)
    mean = jnp.mean(o, axis=-1, keepdims=True)
    var = jnp.mean(jnp.square(o - mean), axis=-1, keepdims=True)
    o = ((o - mean) * lax.rsqrt(var + GN_EPS)).reshape(b, t, D_RWKV) * ln_x_w + ln_x_b
    bonus = jnp.sum(rh * kh * r_k, axis=-1, keepdims=True) * vh
    o_rwkv = ((o + bonus.reshape(b, t, D_RWKV)) * g).astype(x.dtype)

    o_pool, new_pool = _pool_mixer(u, pool_prev, start_pos, pool_map, pool_scale)

    merged = (gate_rwkv * (o_rwkv @ w_branch_rwkv)
              + gate_pool * (o_pool.astype(x.dtype) @ w_branch_pool))
    x = x + _rmsnorm(merged @ w_out, g_mix_post)
    h = _rmsnorm(x, g_ffn_pre)
    gt, up = jnp.split(h @ w_ffn_in, 2, axis=-1)
    x = x + _rmsnorm((jax.nn.silu(gt) * up) @ w_ffn_out, g_ffn_post)
    return x, v_first, ps[:, -1].astype(shift_prev.dtype), s_new.astype(wkv_prev.dtype), new_pool

def setup_inputs(seed: int = 0) -> dict:
    key = jax.random.key(seed)
    ks = jax.random.split(key, 32)
    f32 = jnp.float32
    nrm = lambda kk, shape, scale: jax.random.normal(kk, shape, f32) * scale
    gain = lambda kk, shape: 1.0 + 0.05 * jax.random.normal(kk, shape, f32)
    return {
        'x_prompt': nrm(ks[0], (BATCH, SEQ, D_MODEL), 1.0),
        'x_sample': nrm(ks[1], (DEC_BATCH, DEC_SEQ, D_MODEL), 1.0),
        'state_wkv': nrm(ks[2], (DEPTH, DEC_BATCH, N_HEADS, HEAD_DIM, HEAD_DIM), 0.3),
        'state_shift': nrm(ks[3], (DEPTH, DEC_BATCH, D_SHIFT), 1.0),
        'state_pool': nrm(ks[4], (DEPTH, DEC_BATCH, POOL_BUF, D_POOL), 1.0),
        'norm_mix_pre': gain(ks[5], (DEPTH, D_MODEL)),
        'norm_mix_post': gain(ks[6], (DEPTH, D_MODEL)),
        'norm_ffn_pre': gain(ks[7], (DEPTH, D_MODEL)),
        'norm_ffn_post': gain(ks[8], (DEPTH, D_MODEL)),
        'w_in': nrm(ks[9], (DEPTH, D_MODEL, D_IN), D_MODEL ** -0.5),
        'mu_shift': jax.random.uniform(ks[10], (DEPTH, D_SHIFT), f32),
        'decay_bias': jax.random.uniform(ks[11], (DEPTH, D_RWKV), f32, -6.0, -1.0),
        'w_decay_up': nrm(ks[12], (DEPTH, LORA_DECAY, D_RWKV), 0.1),
        'iclr_bias': nrm(ks[13], (DEPTH, D_RWKV), 0.5),
        'w_iclr_up': nrm(ks[14], (DEPTH, LORA_ICLR, D_RWKV), LORA_ICLR ** -0.5),
        'w_gate_up': nrm(ks[15], (DEPTH, LORA_GATE, D_RWKV), LORA_GATE ** -0.5),
        'k_k': 0.85 + nrm(ks[16], (DEPTH, D_RWKV), 0.05),
        'k_a': gain(ks[17], (DEPTH, D_RWKV)),
        'r_k': nrm(ks[18], (DEPTH, N_HEADS, HEAD_DIM), 0.1),
        'ln_x_w': gain(ks[19], (DEPTH, D_RWKV)),
        'ln_x_b': nrm(ks[20], (DEPTH, D_RWKV), 0.02),
        'vres_bias': nrm(ks[21], (DEPTH - 1, D_RWKV), 0.5),
        'w_vres_down': nrm(ks[22], (DEPTH - 1, D_MODEL, LORA_VRES), D_MODEL ** -0.5),
        'w_vres_up': nrm(ks[23], (DEPTH - 1, LORA_VRES, D_RWKV), LORA_VRES ** -0.5),
        'pool_map': nrm(ks[24], (DEPTH, N_POOL_GROUPS, POOL_GROUP_DIM, POOL_GROUP_DIM), POOL_GROUP_DIM ** -0.5),
        'pool_scale': gain(ks[25], (DEPTH, D_POOL)),
        'w_branch_rwkv': nrm(ks[26], (DEPTH, D_RWKV, D_MODEL), D_RWKV ** -0.5),
        'w_branch_pool': nrm(ks[27], (DEPTH, D_POOL, D_MODEL), D_POOL ** -0.5),
        'w_out': nrm(ks[28], (DEPTH, D_MODEL, D_MODEL), D_MODEL ** -0.5),
        'w_ffn_in': nrm(ks[29], (DEPTH, D_MODEL, 2 * D_FF), D_MODEL ** -0.5),
        'w_ffn_out': nrm(ks[30], (DEPTH, D_FF, D_MODEL), D_FF ** -0.5),
    }

def reference(x_prompt, x_sample, state_wkv, state_shift, state_pool,
              norm_mix_pre, norm_mix_post, norm_ffn_pre, norm_ffn_post,
              w_in, mu_shift, decay_bias, w_decay_up, iclr_bias, w_iclr_up, w_gate_up,
              k_k, k_a, r_k, ln_x_w, ln_x_b, vres_bias, w_vres_down, w_vres_up,
              pool_map, pool_scale, w_branch_rwkv, w_branch_pool, w_out, w_ffn_in, w_ffn_out):
    b_p = x_prompt.shape[0]
    wkv0 = jnp.zeros((b_p, N_HEADS, HEAD_DIM, HEAD_DIM), state_wkv.dtype)
    shift0 = jnp.zeros((b_p, D_SHIFT), state_shift.dtype)
    pool0 = jnp.zeros((b_p, POOL_BUF, D_POOL), state_pool.dtype)
    y_p, y_s = x_prompt, x_sample
    vf_p, vf_s = None, None
    wkv_p, shift_p, pool_p = [], [], []
    wkv_s, shift_s, pool_s = [], [], []
    for l in range(DEPTH):
        lw = (norm_mix_pre[l], norm_mix_post[l], norm_ffn_pre[l], norm_ffn_post[l], w_in[l],
              mu_shift[l], decay_bias[l], w_decay_up[l], iclr_bias[l], w_iclr_up[l], w_gate_up[l],
              k_k[l], k_a[l], r_k[l], ln_x_w[l], ln_x_b[l], pool_map[l], pool_scale[l],
              w_branch_rwkv[l], w_branch_pool[l], w_out[l], w_ffn_in[l], w_ffn_out[l])
        vres = None if l == 0 else (vres_bias[l - 1], w_vres_down[l - 1], w_vres_up[l - 1])
        y_p, vf_p, sh, wk, pl = _block(y_p, shift0, wkv0, pool0, 0, vf_p, vres, lw)
        wkv_p.append(wk)
        shift_p.append(sh)
        pool_p.append(pl)
        y_s, vf_s, sh, wk, pl = _block(y_s, state_shift[l], state_wkv[l], state_pool[l],
                                       PAST_LEN, vf_s, vres, lw)
        wkv_s.append(wk)
        shift_s.append(sh)
        pool_s.append(pl)
    return (y_p, y_s,
            jnp.stack(wkv_p), jnp.stack(shift_p), jnp.stack(pool_p),
            jnp.stack(wkv_s), jnp.stack(shift_s), jnp.stack(pool_s))


_drawn_inputs = setup_inputs


def setup_inputs(seed=0):
    import zlib

    import numpy as np

    out = dict(_drawn_inputs(seed))
    spreads = {}
    factors = {'ln_x_w': 2.899, 'ln_x_b': 6.808}
    for name, (base, spread) in spreads.items():
        noise = np.random.default_rng([zlib.crc32(name.encode()), seed]).standard_normal(out[name].shape)
        drawn = base * np.exp(spread * noise) if base else spread * noise
        out[name] = __import__('jax').numpy.asarray(drawn.astype(out[name].dtype))
    for name, factor in factors.items():
        out[name] = (out[name] * factor).astype(out[name].dtype)
    return out
```

```python
from contextlib import ExitStack

import concourse.bass as bass
import numpy as np
from concourse import mybir

F32 = mybir.dt.float32
F32R = mybir.dt.float32r
F16 = mybir.dt.float16
U32 = mybir.dt.uint32
ALU = mybir.AluOpType
ACT = mybir.ActivationFunctionType
AX = mybir.AxisListType.X

P = 128
D = 1024
KB = D // P
TP = 2048
NSEQ, LSEQ = 8, 8
TS = NSEQ * LSEQ
TT = TP + TS
NT = TP // P
H, HD = 12, 64
DR = H * HD
RB = DR // P
WC = 256
NSH = 20
NFM = 22
NGB = 8
FF = 2816
FB = FF // P
EPS = 1e-6
GN_EPS = 1e-5 * HD
HIST = 15
LOGW = -0.6065306597126334
GROUPS = [(512 * g, 512) for g in range(4)] + [(TP, TS)]
EWIDTH = -(-TT // (5 * LSEQ)) * LSEQ
EVEN = [(EWIDTH * g, min(EWIDTH, TT - EWIDTH * g)) for g in range(5)]


def split3(pe, out, lhs, rhs, first, last):
    pe.matmul(out, lhs[0], rhs[0], start=first, stop=False)
    pe.matmul(out, lhs[0], rhs[1], start=False, stop=False)
    return pe.matmul(out, lhs[1], rhs[0], start=False, stop=last)


CREDIT = 2


def done(n):
    return n + 1 + CREDIT


def landed(n):
    return 16 * n + 16 + 16 * CREDIT


class Scope:

    def __init__(self, nc, ctx, tag):
        self.nc, self.ctx, self.tag, self.credits = nc, ctx, tag, []

    def sb(self, name, shape, dt=F32):
        return self.ctx.enter_context(self.nc.sbuf_tensor(f"{self.tag}_{name}", shape, dt))

    def ps(self, name, shape, dt=F32):
        return self.ctx.enter_context(self.nc.psum_tensor(f"{self.tag}_{name}", shape, dt))

    def sem(self, name, unit=1):
        s = self.nc.alloc_semaphore(f"{self.tag}_{name}")
        self.credits.append((s, unit * CREDIT))
        return s

    def start(self):
        with self.nc.Block() as begin:
            @begin.gpsimd
            def _(pool):
                for s, n in self.credits:
                    pool.sem_inc(s, n)
        self.ctx.callback(self.nc.clear_and_free_semaphores, [s for s, _ in self.credits])
        return self.ctx.enter_context(self.nc.Block())


def phase_a(nc, io, dr):
    with ExitStack() as ctx:
        m = Scope(nc, ctx, "a")
        xh = m.sb("xh", [P, KB, TT], F32R)
        xl = m.sb("xl", [P, KB, TT], F32R)
        wraw = m.sb("wraw", [P, 2, KB, WC])
        wh = m.sb("wh", [P, 2, KB, WC], F32R)
        wl = m.sb("wl", [P, 2, KB, WC], F32R)
        xs = m.sb("xs", [P, 3, KB, P])
        rstd_row = xs[:].rearrange("p a k t -> p (a k t)")[:, 0:TT]
        rstd = m.sb("rstd", [P, NT + 1])
        mhalf = m.sb("mhalf", [P, NT + 1])
        raw = m.sb("raw", [P, 2, 513])
        dif = m.sb("dif", [P, 512])
        out = m.sb("out", [P, 2, 512])
        sq = (xs[:, 2], out[:].rearrange("p a (k t) -> p (a k) t", k=KB // 2))
        ones = m.sb("ones", [P, 1])
        ident = m.sb("ident", [P, P])
        ones_row = m.sb("ones_row", [P, P])
        gpre = m.sb("gpre", [P, KB])
        mu = m.sb("mu", [P, NSH])
        stshift = m.sb("stshift", [P, NSH, NSEQ])
        shp = m.sb("shp", [P, NSH])
        shs = m.sb("shs", [P, NSH, NSEQ])
        pp = m.ps("pp", [P, 2, 512])
        pss = m.ps("pss", [P, 2, 512])

        cons = m.sem("consts", 16)
        x_in = [m.sem(f"x_in{u}", 16) for u in range(2)]
        ones_set = m.sem("ones_set")
        sq_done, fold_done, ss_done, rstd_done = m.sem("sq_done"), m.sem("fold_done"), m.sem("ss_done"), m.sem("rstd_done")
        ms_done, diag_done, row_done, row_kept = m.sem("ms_done"), m.sem("diag_done"), m.sem("row_done"), m.sem("row_kept")
        xh_done, xl_done = m.sem("xh_done"), m.sem("xl_done")
        w_in = [m.sem(f"w_in{u}", 16) for u in range(2)]
        wg_done, wh_done, wl_done = m.sem("wg_done"), m.sem("wh_done"), m.sem("wl_done")
        proj_done = m.sem("proj_done")
        evac_done = m.sem("evac_done")
        dif_done, mixed_done = m.sem("dif_done"), m.sem("mixed_done")
        stored = [m.sem(f"stored{s}", 16) for s in range(2)]
        kept_out = m.sem("kept_out", 16)
        block = m.start()

        NPIECE = NT + 1
        groups = EVEN
        NG = len(groups)
        JB = 2 * NG
        NFB = NFM // 2
        NJ = NFB * JB
        GT = NT + 1
        NJALL = NJ + NGB * GT
        size = lambda q: P if q < NT else TS

        @block.sync
        def _(sp):
            sp.dma_start(gpre[:], io["gpreT"]).then_inc(cons, 16)
            sp.dma_start(mu[:], io["muT"]).then_inc(cons, 16)
            sp.dma_start(stshift[:], io["stshiftT"]).then_inc(cons, 16)
            sp.dma_start(ident[:], io["ident"]).then_inc(cons, 16)
            for u in range(2):
                sp.dma_start(wraw[:, u], io["w_in"][u]).then_inc(w_in[u], 16)
            for q in range(NPIECE):
                sp.wait_ge(xl_done, done(q - 2))
                sp.wait_ge(sq_done, done(q - 2))
                n = size(q)
                sp.dma_start(xs[:, q % 2, :, 0:n], io["xT"][q, :, :, 0:n]).then_inc(x_in[q % 2], 16)

            def load_w(b, u):
                sp.wait_ge(wl_done, done(b - 2))
                sp.dma_start(wraw[:, u], io["w_in"][b]).then_inc(w_in[u], 16)

            def store_fm(b, fb, g, ready=mixed_done):
                j = fb * NG + g
                t0, n = groups[g]
                sp.wait_ge(ready, done(b * JB + j))
                sp.dma_start(dr["fm"][:, 2 * b + fb, t0:t0 + n], out[:, j % 2, 0:n]).then_inc(stored[j % 2], 16)

            with sp.Fori(0, 5) as i:
                for u in range(2):
                    load_w(2 * i + u + 2, u)
                    for fb in range(2):
                        for g in range(NG):
                            store_fm(2 * i + u, fb, g)
            load_w(12, 0)
            for fb in range(2):
                for g in range(NG):
                    store_fm(10, fb, g, evac_done)
            sp.dma_start(io["o_shp"], shp[:]).then_inc(kept_out, 16)
            sp.dma_start(io["o_shs"], shs[:]).then_inc(kept_out, 16)

            def store_gate(c, u, q):
                n, s = size(q), (u * GT + q) % 2
                sp.wait_ge(evac_done, done(NJ + c * GT + q))
                sp.dma_start(dr["gate"][q * P:q * P + n, bass.ds(c * WC, WC)], out[0:n, s, 0:WC]).then_inc(stored[s], 16)

            with sp.Fori(0, 3) as i:
                for u in range(2):
                    load_w(2 * i + u + 13, (u + 1) % 2)
                    for q in range(GT):
                        store_gate(2 * i + u, u, q)
            for c in (6, 7):
                for q in range(GT):
                    store_gate(c, c % 2, q)
            sp.wait_ge(kept_out, landed(1))
            for s in range(2):
                sp.wait_ge(stored[s], landed(NJALL // 2 - 1))

        @block.gpsimd
        def _(pool):
            pool.memset(ones[:], 1.0 / D).then_inc(ones_set, 1)
            pool.memset(ones_row[:], 1.0).then_inc(ones_set, 1)
            pool.wait_ge(cons, landed(3))

            def gain(b, u, k):
                pool.wait_ge(w_in[u], landed(k))
                pool.tensor_tensor(wraw[:, u], wraw[:, u], gpre[:, :, None].broadcast_to([P, KB, WC]), ALU.mult).then_inc(wg_done, 1)
            gain(0, 0, 0)
            pool.memset(mhalf[:], -0.5).then_inc(ones_set, 1)
            pool.wait_ge(ones_set, done(2))
            pool.wait_ge(ms_done, done(0))
            pool.tensor_tensor(rstd[:], rstd[:], mhalf[:], ALU.pow).then_inc(rstd_done, 1)
            with pool.Fori(0, 9) as i:
                gain(2 * i + 1, 1, i)
                gain(2 * i + 2, 0, i + 1)

        def last_job(b):
            return b * JB + JB - 1 if not isinstance(b, int) or b < NFB else NJ + (b - NFB) * GT + GT - 1

        def hi_w(act, b, u, before):
            act.wait_ge(proj_done, done(before))
            act.wait_ge(wg_done, done(b))
            act.activation(wh[:, u], wraw[:, u], ACT.Copy).then_inc(wh_done, 1)

        @block.scalar
        def _(act):
            hi_w(act, 0, 0, -2)

            for q in range(NPIECE):
                n = size(q)
                act.wait_ge(x_in[q % 2], landed(q // 2))
                act.activation(xh[:, :, q * P:q * P + n], xs[:, q % 2, :, 0:n], ACT.Copy).then_inc(xh_done, 1)
                act.wait_ge(ss_done, done(q - 2))
                act.activation(sq[q % 2][:, :, 0:n], xs[:, q % 2, :, 0:n], ACT.Square).then_inc(sq_done, 1)
            for g, (t0, n) in enumerate(GROUPS):
                act.wait_ge(row_done, done(g))
                act.activation(rstd_row[:, t0:t0 + n], pss[:, 1, 0:n], ACT.Copy).then_inc(row_kept, 1)

            with act.Fori(0, 5) as i:
                for u in range(2):
                    hi_w(act, 2 * i + u + 1, 1 - u, (2 * i + u) * JB - 1)
            hi_w(act, 11, 1, last_job(9))

            def gate(c, u, q, k):
                s, n = (u * GT + q) % 2, size(q)
                act.wait_ge(stored[s], landed(NJ // 2 + k - 1))
                act.wait_ge(proj_done, done(NJ + c * GT + q))
                act.activation(out[0:n, s, 0:WC], pp[0:n, s, 0:WC], ACT.Sigmoid,
                               scale=rstd[0:n, q:q + 1]).then_inc(evac_done, 1)
            hi_w(act, 12, 0, last_job(10))
            act.wait_ge(rstd_done, done(0))
            act.wait_ge(evac_done, done(NJ - 1))
            for q in range(GT):
                gate(0, 0, q, q // 2)
            with act.Fori(0, 3) as i:
                for u in range(2):
                    hi_w(act, 2 * i + u + 13, 1 - u, NJ + (2 * i + u) * GT + GT - 1)
                    for q in range(GT):
                        gate(2 * i + u + 1, 1 - u, q, i * GT + ((u + 1) * GT + q) // 2)
            for q in range(GT):
                gate(7, 1, q, (7 * GT + q) // 2)

        def lo_w(dve, b, u):
            dve.wait_ge(wh_done, done(b))
            dve.tensor_tensor(wl[:, u], wraw[:, u], wh[:, u].bitcast(F32), ALU.subtract).then_inc(wl_done, 1)

        @block.vector
        def _(dve):
            lo_w(dve, 0, 0)

            for q in range(NPIECE):
                n = size(q)
                dve.wait_ge(xh_done, done(q))
                dve.tensor_tensor(xl[:, :, q * P:q * P + n], xs[:, q % 2, :, 0:n],
                                  xh[:, :, q * P:q * P + n].bitcast(F32), ALU.subtract).then_inc(xl_done, 1)
                dve.wait_ge(sq_done, done(q))
                for i, w in enumerate((4, 2)):
                    v = sq[q % 2]
                    dve.tensor_tensor(v[:, 0:w, 0:n], v[:, 0:w, 0:n], v[:, w:2 * w, 0:n], ALU.add).then_inc(fold_done, 1)
                    dve.wait_ge(fold_done, done(2 * q + i))
            dve.wait_ge(ss_done, done(NPIECE - 1))
            dve.tensor_scalar(rstd[:, 0:NT], pss[:, 0, 0:NT], EPS, None, ALU.add)
            dve.memset(rstd[TS:P, NT:NT + 1], 1.0)
            dve.tensor_scalar(rstd[0:TS, NT:NT + 1], pss[0:TS, 0, NT:NT + 1], EPS, None, ALU.add).then_inc(ms_done, 1)
            dve.wait_ge(cons, landed(3))
            dve.wait_ge(rstd_done, done(0))
            for g, (t0, n) in enumerate(GROUPS):
                dve.wait_ge(row_done, done(g - 1))
                for a in range(max(n // P, 1)):
                    w = min(n, P)
                    ins = dve.tensor_scalar(dif[0:w, a * P:a * P + w], ident[0:w, 0:w], rstd[0:w, t0 // P + a:t0 // P + a + 1],
                                            None, ALU.mult)
                ins.then_inc(diag_done, 1)
            dve.wait_ge(cons, landed(3))

            def mix(b, fb, g):
                j = fb * NG + g
                s, (t0, n), f = j % 2, groups[g], 2 * b + fb
                job = b * JB + j
                npr = min(n, TP - t0)
                if g == 0:
                    dve.memset(raw[:, s, 0:1], 0.0)
                else:
                    w = groups[g - 1][1]
                    dve.tensor_copy(raw[:, s, 0:1], raw[:, 1 - s, w:w + 1])
                dve.wait_ge(proj_done, done(job))
                dve.tensor_tensor(raw[:, s, 1:1 + n], pp[:, s, 0:n], rstd_row[:, t0:t0 + n], ALU.mult).then_inc(evac_done, 1)
                dve.wait_ge(evac_done, done(job))
                dve.tensor_tensor(dif[:, 0:npr], raw[:, s, 0:npr], raw[:, s, 1:npr + 1], ALU.subtract).then_inc(dif_done, 1 if npr < n else 3)
                if npr < n:
                    dve.tensor_copy(shp[:, bass.ds(f, 1)], raw[:, s, npr:npr + 1])
                    d3 = dif[:, npr:n].rearrange("p (s l) -> p s l", l=LSEQ)
                    r3 = raw[:, s, npr + 1:n + 1].rearrange("p (s l) -> p s l", l=LSEQ)
                    dve.tensor_tensor(d3[:, :, 1:], r3[:, :, :-1], r3[:, :, 1:], ALU.subtract).then_inc(dif_done, 1)
                    st = stshift[:, bass.ds(f, 1), :].rearrange("p a s -> p (a s)")
                    dve.tensor_tensor(d3[:, :, 0], st, r3[:, :, 0], ALU.subtract).then_inc(dif_done, 1)
                    dve.tensor_copy(shs[:, bass.ds(f, 1), :].rearrange("p a s -> p (a s)"), r3[:, :, LSEQ - 1])
                dve.wait_ge(stored[s], landed(b * NG + j // 2 - 1))
                dve.wait_ge(dif_done, 3 * (job + 1) + CREDIT)
                dve.scalar_tensor_tensor(out[:, s, 0:n], dif[:, 0:n], mu[:, bass.ds(f, 1)], raw[:, s, 1:1 + n],
                                         ALU.mult, ALU.add).then_inc(mixed_done, 1)
            with dve.Fori(0, 5) as i:
                for u in range(2):
                    lo_w(dve, 2 * i + u + 1, 1 - u)
                    for fb in range(2):
                        for g in range(NG):
                            mix(2 * i + u, fb, g)
            lo_w(dve, 11, 1)
            for fb in range(2):
                for g, (t0, n) in enumerate(groups):
                    j = fb * NG + g
                    dve.wait_ge(stored[j % 2], landed(10 * NG + j // 2 - 1))
                    dve.wait_ge(proj_done, done(10 * JB + j))
                    dve.tensor_tensor(out[:, j % 2, 0:n], pp[:, j % 2, 0:n], rstd_row[:, t0:t0 + n], ALU.mult).then_inc(evac_done, 1)
            for b in range(12, NFB + NGB):
                lo_w(dve, b, b % 2)

        @block.tensor
        def _(pe):
            pe.wait_ge(ones_set, done(1))
            for q in range(NPIECE):
                n = size(q)
                pe.wait_ge(fold_done, done(2 * q + 1))
                for k in range(2):
                    mm = pe.matmul(pss[0:n, 0, q:q + 1], sq[q % 2][:, k, 0:n], ones[:, 0:1], start=k == 0, stop=k == 1)
                mm.then_inc(ss_done, 1)
            for g, (t0, n) in enumerate(GROUPS):
                pe.wait_ge(row_kept, done(g - 1))
                pe.wait_ge(diag_done, done(g))
                w = min(n, P)
                pe.matmul(pss[:, 1, 0:n], ones_row[0:w], dif[0:w, 0:n], start=True, stop=True).then_inc(row_done, 1)
            pe.wait_ge(xl_done, done(NPIECE - 1))

            def fm_block(b, u):
                pe.wait_ge(wl_done, done(b))
                for fb in range(2):
                    for g, (t0, n) in enumerate(groups):
                        j = fb * NG + g
                        pe.wait_ge(evac_done, done(b * JB + j - 2))
                        w, x = slice(fb * P, fb * P + P), slice(t0, t0 + n)
                        for k in range(KB):
                            mm = split3(pe, pp[:, j % 2, 0:n], (wh[:, u, k, w], wl[:, u, k, w]),
                                        (xh[:, k, x], xl[:, k, x]), k == 0, k == KB - 1)
                        mm.then_inc(proj_done, 1)

            def gate_block(c, u):
                pe.wait_ge(wl_done, done(NFB + c))
                for q in range(GT):
                    g, n = u * GT + q, size(q)
                    pe.wait_ge(evac_done, done(NJ + c * GT + q - 2))
                    x = slice(q * P, q * P + n)
                    for k in range(KB):
                        mm = split3(pe, pp[0:n, g % 2, 0:WC], (xh[:, k, x], xl[:, k, x]),
                                    (wh[:, 1 - u, k], wl[:, 1 - u, k]), k == 0, k == KB - 1)
                    mm.then_inc(proj_done, 1)
            with pe.Fori(0, 5) as i:
                for u in range(2):
                    fm_block(2 * i + u, u)
            fm_block(10, 0)
            with pe.Fori(0, 4) as i:
                for u in range(2):
                    gate_block(2 * i + u, u)



def phase_b(nc, io, dr):
    with ExitStack() as ctx:
        m = Scope(nc, ctx, "b")
        wdec = m.sb("wdec", [65, DR])
        wiclr = m.sb("wiclr", [P, DR])
        wgate = m.sb("wgate", [P, DR])
        lnw, lnb = m.sb("lnw", [P, DR]), m.sb("lnb", [P, DR])
        trip, tris = m.sb("trip", [P, P + 1]), m.sb("tris", [TS, NSEQ * (LSEQ + 1)])
        maskp, masks = m.sb("maskp", [P, 4, P], U32), m.sb("masks", [TS, 4, TS], U32)
        lvl, w1 = m.sb("lvl", [P, 6, P]), m.sb("w1", [P, P])
        ident = m.sb("ident", [P, P])
        ident16, nident16 = m.sb("ident16", [P, P], F16), m.sb("nident16", [P, P], F16)
        hsel = m.sb("hsel", [P, 2])
        rk = m.sb("rk", [P, RB, 2])
        kk, ka = m.sb("kk", [P, RB]), m.sb("ka", [P, RB])
        bicl, hbicl = m.sb("bicl", [P, RB]), m.sb("hbicl", [P, RB])
        pmap, pscale = m.sb("pmap", [P, 2, P]), m.sb("pscale", [P, 2])
        cnt0, cnt1 = m.sb("cnt0", [P, 2, P]), m.sb("cnt1", [P, 2, P])
        sel = m.sb("sel", [TS, NSEQ])
        pace = m.sb("pace", [P, H])
        mhalf, gneps = m.sb("mhalf", [P, H]), m.sb("gneps", [P, H])
        fm = m.sb("fm", [P, NSH, P])
        tw = m.sb("tw", [65, P])
        ld = m.sb("ld", [P, DR])
        ic = m.sb("ic", [P, RB, P])
        kn = m.sb("kn", [P, RB, P])
        sq = m.sb("sq", [P, RB, P])
        km = m.sb("km", [P, RB, P])
        be, ke = m.sb("be", [P, RB, P]), m.sb("ke", [P, RB, P])
        rn = m.sb("rn", [P, 2, H])
        lT = m.sb("lT", [P, H, P])
        ph, pl = m.sb("ph", [P, H, P], F16), m.sb("pl", [P, H, P], F16)
        t16, tt16, x16 = (m.sb(x, [P, H, P], F16) for x in ("t16", "tt16", "x16"))
        ar = m.sb("ar", [P, 2, RB, 2, P])
        ep, em = m.sb("ep", [P, 2, RB, P + 1]), m.sb("em", [P, 2, RB, P + 1])
        m3 = m.sb("m3", [P, 2, H, 3, P])
        tt = m.sb("tt", [P, 2, H, P])
        vt, bet, ket = (m.sb(x, [P, 2, DR]) for x in ("vt", "bet", "ket"))
        bon = m.sb("bon", [P, 2, H])
        sg = m.sb("sg", [P, 2, P])
        uf = m.sb("uf", [P, 2, 2, HIST + P])
        st, sc = m.sb("st", [P, RB, HD]), m.sb("sc", [P, RB, HD])
        xu = m.sb("xu", [P, 2, DR])
        oc, on = m.sb("oc", [P, DR]), m.sb("on", [P, DR])
        mv = m.sb("mv", [P, 4, H])
        oT = m.sb("oT", [P, KB, 2, P], F32R)
        pc = m.sb("pc", [P, 2, P])
        ufs = m.sb("ufs", [P, 2, NSEQ, HIST + LSEQ])
        win = m.sb("win", [P, 2, 2, NSEQ * (HIST + LSEQ)])
        tmp = m.sb("tmp", [TS, 2, 512])
        sS = m3[:, 1].rearrange("p h w t -> p (h w t)")[:, 0:RB * NSEQ * HD].rearrange("p (b s d) -> p b s d", b=RB, s=NSEQ)
        spread = ((tmp[:, 0], tmp[:, 1]), tuple(x[0:TS].rearrange("p b t -> p (b t)")[:, 0:512] for x in (kn, km)))
        pA, pB, pC, pD = (m.ps(x, [P, 2, 512]) for x in ("pA", "pB", "pC", "pD"))

        cons = m.sem("consts", 16)
        f_in, u_in, st_in = m.sem("f_in", 16), m.sem("u_in", 16), m.sem("s_in", 16)
        o_st = m.sem("o_stored", 16)
        keep_st = m.sem("kept_stored", 16)
        turn = {e: m.sem(f"turn_{e}") for e in ("pe", "act", "dve", "pool")}
        S = {x: m.sem(x) for x in (
            "const_set ones_row hb tw tg tz ld z a ss ssc rn rb rt kq sq tha ic f km kn al re bt be ke rkp "
            "c ep em vt vts bet bets ket kets bonus bonc ah am pht plt t2t t2 t2s p1 xm tp tpt tc ttc nr rr nt ttf "
            "s0c x xs u us o mean nmean oc sqo var veps rs onr lw bv lb onb ds dsa sn g og ot oh ol "
            "hist pdiff pmm plh pll sgm fs fr fx fo fu fd fda sS").split()}
        block = m.start()

        def bank(p, s, n):
            return p[0:n, s].rearrange("p (h t) -> p h t", h=4)[:, :, 0:n]

        def bank16(g, n):
            return pB[0:n, g % 2].bitcast(F16)[:, 0:512].rearrange("p (h t) -> p h t", h=4)[:, :, 0:n]

        def halves(p, n=P):
            return p[0:n, :, 0:384]

        def cut(a, n=P):
            return a[0:n].rearrange("p (c k) -> p c k", c=2)

        def parity(a, n=P):
            return a[0:n].rearrange("p (b c d) -> p c b d", c=2, d=HD)

        def odd_even(p, n=P):
            return p[0:n, :, 0:384].rearrange("p c (b d) -> p c b d", d=HD)

        def heads(a, n=P):
            return a[0:n].rearrange("p (h d) -> p h d", h=H)

        def blk(p, b, n=P, w=P, q=P):
            return p[0:q, b // 3, (b % 3) * w:(b % 3) * w + n]

        def seg(a, n, first, width):
            if n == P:
                return a[:, :, first:first + n]
            return a[:, :, 0:NSEQ * (LSEQ + 1)].rearrange("p b (s l) -> p b s l", s=NSEQ)[:, :, :, first:first + LSEQ]

        def tok(a, n):
            return a[:, :, 0:n] if n == P else a[:, :, 0:n].rearrange("p b (s l) -> p b s l", s=NSEQ)

        levels = lambda n: range(6) if n == P else range(2)
        NL = 6
        lix = lambda t, l, g: (t * NL + l) * 3 + g

        def begin(eng, me, t):
            for e, s in turn.items():
                if e != me:
                    eng.wait_ge(s, done(t - 1))

        def turns(eng, body, peeled=0):
            body(0, 0, P)
            body(1, 1, P)
            with eng.Fori(0, NT // 2 - 1 - peeled // 2) as i:
                body(2 * i + 2, 0, P)
                body(2 * i + 3, 1, P)
            for t in range(NT - peeled, NT):
                body(t, t % 2, P)
            body(NT, 0, TS)
            body(NT + 1, 1, 0)

        def cols(t, n):
            return slice(t * P, t * P + n) if isinstance(t, int) else bass.ds(t * P, n)

        def has1(t):
            return not isinstance(t, int) or t <= NT

        def has2(t):
            return not isinstance(t, int) or t >= 1

        def size2(t):
            return TS if isinstance(t, int) and t == NT + 1 else P

        CONSTS = (("wdec", wdec), ("wgate", wgate), ("lnw", lnw), ("lnb", lnb), ("trip", trip), ("tris", tris),
                  ("lvl", lvl), ("w1", w1), ("ident", ident), ("hsel", hsel), ("rk", rk), ("kk", kk), ("ka", ka),
                  ("bicl", bicl), ("pmap", pmap), ("pscale", pscale), ("cnt0", cnt0), ("cnt1", cnt1), ("sel", sel))
        NCONST = len(CONSTS) + 3

        @block.sync
        def _(sp):
            sp.dma_start(fm[:], dr["fm"][:, 0:NSH, 0:P]).then_inc(f_in, 16)
            for name, dst in CONSTS:
                sp.dma_start(dst[:], io[name]).then_inc(cons, 16)
            sp.dma_start(wiclr[64:P], io["wiclr"]).then_inc(cons, 16)
            sp.dma_start(maskp[:], io["maskp"]).then_inc(cons, 16)
            sp.dma_start(masks[:], io["masks"]).then_inc(cons, 16)

            def body(t, u, n):
                begin(sp, "sp", t)
                if isinstance(t, int) and t == NT + 1:
                    sp.dma_start(sS, io["s0"]).then_inc(st_in, 16)
                    sp.wait_ge(u_in, landed(NT + 3))
                    sp.dma_start(io["o_pools"], ufs[:, :, :, LSEQ:LSEQ + HIST]).then_inc(keep_st, 16)
                if has1(t) and n == P:
                    sp.dma_start(uf[:, u, :, HIST:], dr["fm"][:, NSH:NFM, cols(t, P)]).then_inc(u_in, 16)
                elif n == TS:
                    sp.wait_ge(u_in, landed(NT - 1))
                    sp.dma_start(io["o_poolp"], uf[:, 1, :, P:P + HIST]).then_inc(keep_st, 16)
                    for b in range(2):
                        sp.dma_start(ufs[:, b, :, HIST:], dr["fm"][:, NSH + b, TP:TT].rearrange("p (s l) -> p s l", s=NSEQ)).then_inc(u_in, 16)
                        sp.dma_start(ufs[:, b, :, 0:HIST], io["pool0"][:, b]).then_inc(u_in, 16)
                if has1(t) and not (isinstance(t, int) and t == NT):
                    for r in ("re", "rkp", "vt", "a", "kq", "tw", "tg", "km"):
                        sp.wait_ge(S[r], done(t))
                    nn = TS if isinstance(t, int) and t == NT - 1 else P
                    sp.dma_start(fm[:, :, 0:nn], dr["fm"][:, 0:NSH, cols(t + 1, nn)]).then_inc(f_in, 16)
                if has2(t):
                    n2 = size2(t)
                    sp.wait_ge(S["ol"], done(t - 1))
                    sp.wait_ge(S["pll"], done(t - 1))
                    sp.dma_start(dr["o"][t - 1, :, :, :, 0:n2], oT[:, :, :, 0:n2].bitcast(F32)).then_inc(o_st, 16)
                if isinstance(t, int) and t == NT:
                    sp.wait_ge(S["sn"], done(NT - 1))
                    sp.dma_start(io["o_wkvp"], st[:]).then_inc(keep_st, 16)
                if isinstance(t, int) and t == NT + 1:
                    sp.wait_ge(S["sS"], done(RB - 1))
                    sp.dma_start(io["o_wkvs"], sS).then_inc(keep_st, 16)
            turns(sp, body, peeled=2)
            sp.wait_ge(keep_st, landed(3))
            sp.wait_ge(o_st, landed(NT))


        @block.gpsimd
        def _(pool):
            pool.memset(mhalf[:], -0.5).then_inc(S["const_set"], 1)
            pool.memset(gneps[:], GN_EPS).then_inc(S["const_set"], 1)
            pool.memset(uf[:, 1], 0.0).then_inc(S["const_set"], 1)
            pool.wait_ge(S["const_set"], done(2))
            pool.wait_ge(cons, landed(NCONST - 1))

            def body(t, u, n):
                begin(pool, "pool", t)
                if has1(t):
                    pool.wait_ge(S["ssc"], done(t))
                    pool.tensor_tensor(rn[0:n, 1], rn[0:n, 0], mhalf[0:n], ALU.pow).then_inc(S["rn"], 1)
                if has2(t):
                    mix_windows(t, 1 - u, size2(t))
                if has1(t):
                    pool.wait_ge(S["km"], done(t))
                    pool.tensor_tensor(sq[:, :, 0:n], fm[:, 0:RB, 0:n], km[:, :, 0:n], ALU.mult).then_inc(S["rkp"], 1)
                    if n == P:
                        pool.tensor_copy(uf[:, u, :, 0:HIST], uf[:, 1 - u, :, P:P + HIST]).then_inc(S["hist"], 1)
                if has2(t):
                    n2, q, u2 = size2(t), t - 1, 1 - u
                    if n2 == TS:
                        pool.wait_ge(S["us"], done(q))
                    else:
                        pool.wait_ge(S["u"], done(q))
                    pool.tensor_tensor(heads(xu[:, 0], n2), heads(vt[:, u2], n2),
                                       bon[0:n2, u2, :, None].broadcast_to([n2, H, HD]), ALU.mult).then_inc(S["bv"], 1)
                    pool.wait_ge(S["bv"], done(q))
                    pool.tensor_tensor(xu[0:n2, 0], xu[0:n2, 0], lnb[0:n2], ALU.add).then_inc(S["lb"], 1)
                    pool.wait_ge(S["var"], done(q))
                    pool.tensor_tensor(mv[0:n2, 2], mv[0:n2, 2], gneps[0:n2], ALU.add).then_inc(S["veps"], 1)
                    pool.wait_ge(S["veps"], done(q))
                    pool.tensor_tensor(mv[0:n2, 3], mv[0:n2, 2], mhalf[0:n2], ALU.pow).then_inc(S["rs"], 1)
                if has1(t):
                    low_part(t, 0, n)
                if has2(t):
                    pool.wait_ge(S["onr"], done(q))
                    pool.tensor_tensor(on[0:n2], on[0:n2], lnw[0:n2], ALU.mult).then_inc(S["lw"], 1)
                    pool.wait_ge(S["lw"], done(q))
                    pool.wait_ge(S["lb"], done(q))
                    pool.tensor_tensor(on[0:n2], on[0:n2], xu[0:n2, 0], ALU.add).then_inc(S["onb"], 1)
                if has1(t):
                    low_part(t, 1, n)
                    low_part(t, 2, n)
                pool.drain().then_inc(turn["pool"], 1)

            def low_part(t, g, n):
                hs = slice(4 * g, 4 * g + 4)
                pool.wait_ge(S["pht"], done(3 * t + g))
                pool.tensor_tensor(pl[0:n, hs, 0:n], lT[0:n, hs, 0:n], ph[0:n, hs, 0:n], ALU.subtract).then_inc(S["plt"], 1)

            def mix_windows(t, u2, n2):
                q = t - 1
                first = isinstance(q, int) and q == 0
                src, count, ns, ln = (uf[:, u2].rearrange("p b (s l) -> p b s l", s=1), cnt0 if first else cnt1, 1, P) if n2 == P else (ufs[:], cnt1, NSEQ, LSEQ)
                length = HIST + ln
                buf = win[:, :, :, 0:ns * length].rearrange("p w b (s l) -> p w b s l", s=ns)
                prev = src
                if isinstance(q, int) and q == NT:
                    pool.wait_ge(u_in, landed(NT + 3))
                else:
                    pool.wait_ge(u_in, landed(q))
                    pool.wait_ge(S["hist"], done(q))
                for w in range(4):
                    step = 1 << w
                    lo = (2 << w) - 1
                    for b in range(w // 2, 2):
                        ins = pool.tensor_tensor(buf[:, w % 2, b, :, lo:], prev[:, b, :, lo:], prev[:, b, :, lo - step:length - step], ALU.add)
                    ins.then_inc(S["pdiff"], 1)
                    pool.wait_ge(S["pdiff"], done(q * 8 + 2 * w))
                    prev = buf[:, w % 2]
                    b, half = w // 2, w % 2
                    rows = slice(64 * half, 64 * half + 64)
                    dst = pc[rows, b, 0:n2].rearrange("p (s l) -> p s l", s=ns)
                    cn = count[rows, b, 0:n2].rearrange("p (s l) -> p s l", s=ns)
                    pool.tensor_tensor(dst, prev[rows, b, :, HIST:], cn, ALU.mult).then_inc(S["pdiff"], 1)
                    pool.wait_ge(S["pdiff"], done(q * 8 + 2 * w + 1))
                for b in range(2):
                    dst = pc[:, b, 0:n2].rearrange("p (s l) -> p s l", s=ns)
                    pool.tensor_tensor(dst, dst, src[:, b, :, HIST:], ALU.subtract).then_inc(S["fd"], 1)
            turns(pool, body)


        @block.scalar
        def _(act):
            act.wait_ge(cons, landed(NCONST - 1))
            act.activation(hbicl[:], bicl[:], ACT.Copy, scale=0.5).then_inc(S["hb"], 1)
            act.activation(ident16[:], ident[:], ACT.Copy).then_inc(S["hb"], 1)
            act.activation(nident16[:], ident[:], ACT.Copy, scale=-1.0).then_inc(S["hb"], 1)
            act.wait_ge(S["const_set"], done(2))
            act.wait_ge(S["hb"], done(2))

            def body(t, u, n):
                if has1(t):
                    act.wait_ge(f_in, landed(t))
                    act.wait_ge(S["z"], done(t - 1))
                    act.activation(tw[0:64, 0:n], fm[0:64, 18, 0:n], ACT.Tanh).then_inc(S["tw"], 1)
                    act.wait_ge(S["g"], done(t - 2))
                    act.activation(sg[:, u, 0:n], fm[:, 19, 0:n], ACT.Tanh, scale=0.5).then_inc(S["tg"], 1)
                    act.wait_ge(S["bonus"], done(t - 1))
                    act.wait_ge(S["kq"], done(t))
                    act.activation(sq[:, :, 0:n], kn[:, :, 0:n], ACT.Square).then_inc(S["sq"], 1)
                    act.wait_ge(S["c"], done(t - 1))
                    act.wait_ge(S["z"], done(t))
                    act.activation(cut(ld, n), halves(pA, n), ACT.Tanh, scale=0.5).then_inc(S["tz"], 1)
                    act.wait_ge(S["bt"], done(t - 1))
                    act.wait_ge(S["a"], done(t))
                    for b in range(RB):
                        ins = act.activation(ic[:, b, 0:n], blk(pB, b, n), ACT.Tanh, scale=0.5, bias=hbicl[:, b:b + 1])
                    ins.then_inc(S["tha"], 1)
                begin(act, "act", t)
                q, u2, n2 = t - 1, 1 - u, size2(t)
                two = has2(t) and n2 == P
                if has1(t):
                    wd = P + 1 if n == P else NSEQ * (LSEQ + 1)
                    cv = lambda a: a[:, u].rearrange("p (c b) w -> p c b w", c=2)
                    act.wait_ge(S["c"], done(t))
                    for c in range(2):
                        i1 = act.activation(ep[:, u, 3 * c:3 * c + 3, 0:wd], pA[:, c, 0:3 * (P + 1)].rearrange("p (b w) -> p b w", b=3)[:, :, 0:wd], ACT.Exp)
                    i1.then_inc(S["ep"], 1)
                    for c in range(2):
                        i2 = act.activation(em[:, u, 3 * c:3 * c + 3, 0:wd], pA[:, c, 0:3 * (P + 1)].rearrange("p (b w) -> p b w", b=3)[:, :, 0:wd], ACT.Exp, scale=-1.0)
                    i2.then_inc(S["em"], 1)
                    act.wait_ge(S["vt"], done(t))
                    act.activation(cut(vt[:, u], n), halves(pB, n), ACT.Copy).then_inc(S["vts"], 1)
                if has2(t) and not has1(t):
                    squares(act, q, n2)
                if has1(t):
                    act.wait_ge(S["ket"], done(t))
                    act.activation(cut(ket[:, u], n), halves(pB, n), ACT.Copy).then_inc(S["kets"], 1)
                    act.wait_ge(S["bet"], done(t))
                    act.activation(cut(bet[:, u], n), halves(pC, n), ACT.Copy).then_inc(S["bets"], 1)
                    if two:
                        squares(act, q, n2)
                    for g in range(3):
                        act.wait_ge(S["t2"], done(3 * t + g))
                        act.activation(t16[0:n, 4 * g:4 * g + 4, 0:n], bank16(g, n), ACT.Copy).then_inc(S["t2s"], 1)
                    for l in levels(n):
                        for g in range(3):
                            hs = slice(4 * g, 4 * g + 4)
                            act.wait_ge(S["tp"], done(lix(t, l, g)))
                            act.activation(t16[0:n, hs, 0:n], bank(pC, 0, n), ACT.Copy).then_inc(S["tc"], 1)
                            act.wait_ge(S["tpt"], done(lix(t, l, g)))
                            act.activation(tt16[0:n, hs, 0:n], bank(pC, 1, n), ACT.Copy).then_inc(S["ttc"], 1)
                        if has2(t) and l == (3 if n == P else 1):
                            finish(act, t, q, n2)
                elif has2(t):
                    finish(act, t, q, n2)
                act.drain().then_inc(turn["act"], 1)

            def squares(act, q, n2):
                act.wait_ge(S["oc"], done(q))
                act.activation(on[0:n2], oc[0:n2], ACT.Square, scale=HD ** -0.5).then_inc(S["sqo"], 1)

            def finish(act, t, q, n2):
                act.wait_ge(o_st, landed(q - 1))
                act.wait_ge(S["ot"], done(q))
                act.wait_ge(S["pmm"], done(q))
                act.activation(oT[:, 0:3, 0, 0:n2], pD[:, 0, 0:384].rearrange("p (b t) -> p b t", b=3)[:, :, 0:n2], ACT.Copy)
                act.activation(oT[:, 3:6, 0, 0:n2], pD[:, 1, 0:384].rearrange("p (b t) -> p b t", b=3)[:, :, 0:n2], ACT.Copy).then_inc(S["oh"], 1)
                for b in range(2):
                    ins = act.activation(oT[:, 6 + b, 0, 0:n2], pD[:, b, 384:384 + n2], ACT.Copy, scale=pscale[:, b:b + 1])
                ins.then_inc(S["plh"], 1)
            turns(act, body)

        @block.vector
        def _(dve):
            dve.memset(lT[:], 0.0).then_inc(S["ones_row"], 1)
            dve.memset(m3[:], 0.0).then_inc(S["ones_row"], 1)
            dve.memset(st[:], 0.0).then_inc(S["ones_row"], 1)
            dve.memset(tw[64:65], 1.0).then_inc(S["ones_row"], 1)
            dve.wait_ge(cons, landed(NCONST - 1))
            dve.wait_ge(S["hb"], done(2))
            dve.wait_ge(S["ones_row"], done(3))
            bc = lambda a, n: a[:, :, None].broadcast_to([P, RB, n])

            def body(t, u, n):
                if has1(t):
                    if isinstance(t, int) and t == 0:
                        key_scaled(dve, 0)
                    dve.wait_ge(S["tz"], done(t))
                    dve.tensor_scalar(rn[0:n, 0], pA[0:n, 0, 384:384 + H], 1e-24, None, ALU.max).then_inc(S["ssc"], 1)
                    dve.tensor_scalar(ld[0:n], ld[0:n], LOGW / 2, LOGW / 2, ALU.mult, ALU.add).then_inc(S["ld"], 1)
                begin(dve, "dve", t)
                q, u2, n2 = t - 1, 1 - u, size2(t)
                two = has2(t) and n2 == P
                if two:
                    dve.tensor_tensor(sc[:], st[:], em[:, u2, :, 0:1].broadcast_to([P, RB, HD]), ALU.mult).then_inc(S["s0c"], 1)
                if has1(t):
                    dve.wait_ge(S["tg"], done(t))
                    dve.tensor_scalar(sg[:, u, 0:n], sg[:, u, 0:n], 0.5, 0.5, ALU.mult, ALU.add).then_inc(S["sgm"], 1)
                    dve.wait_ge(S["tha"], done(t))
                    dve.tensor_scalar(ic[:, :, 0:n], ic[:, :, 0:n], 0.5, 0.5, ALU.mult, ALU.add).then_inc(S["ic"], 1)
                    dve.wait_ge(S["ic"], done(t))
                    dve.scalar_tensor_tensor(km[:, :, 0:n], ic[:, :, 0:n], -1.0, bc(ka, n), ALU.add, ALU.mult).then_inc(S["f"], 1)
                    dve.wait_ge(S["f"], done(t))
                    dve.wait_ge(S["rn"], done(t))
                    dve.tensor_copy(heads(be[:].rearrange("p b t -> p (b t)"), n), rn[0:n, 1, :, None].broadcast_to([n, H, HD])).then_inc(S["rb"], 1)
                    dve.scalar_tensor_tensor(km[:, :, 0:n], km[:, :, 0:n], 1.0, fm[:, RB:2 * RB, 0:n], ALU.add, ALU.mult).then_inc(S["km"], 1)
                    dve.wait_ge(S["km"], done(t))
                    dve.wait_ge(S["em"], done(t))
                    dve.tensor_tensor(tok(ke, n), tok(km, n), seg(em[:, u], n, 1, 0), ALU.mult).then_inc(S["ke"], 1)
                    dve.wait_ge(S["ep"], done(t))
                    dve.tensor_tensor(tok(ar[:, u, :, 1], n), tok(fm[:, 0:RB], n), seg(ep[:, u], n, 1, 0), ALU.mult).then_inc(S["re"], 1)
                    dve.wait_ge(S["rt"], done(t))
                    for c in range(2):
                        pv = pC[:, c, 0:384].rearrange("p (b t) -> p b t", b=3)[:, :, 0:n]
                        kv = kn[:, 3 * c:3 * c + 3, 0:n]
                        ins = dve.scalar_tensor_tensor(kv, kv, -1.0, pv, ALU.mult, ALU.mult)
                    ins.then_inc(S["kn"], 1)
                    dve.wait_ge(S["kn"], done(t))
                    dve.scalar_tensor_tensor(be[:, :, 0:n], ic[:, :, 0:n], -1.0, kn[:, :, 0:n], ALU.mult, ALU.mult).then_inc(S["bt"], 1)
                    dve.wait_ge(S["bt"], done(t))
                    dve.tensor_tensor(tok(be, n), tok(be, n), seg(em[:, u], n, 1, 0), ALU.mult).then_inc(S["be"], 1)
                    dve.tensor_tensor(tok(ar[:, u, :, 0], n), tok(kn, n), seg(ep[:, u], n, 0, 0), ALU.mult).then_inc(S["al"], 1)
                if two:
                    dve.wait_ge(S["x"], done(q))
                    dve.tensor_copy(parity(xu[:, 0]), odd_even(pD)).then_inc(S["xs"], 1)
                if has1(t):
                    mask = maskp if n == P else masks
                    if n == TS:
                        dve.memset(lT[0:n, :, 0:n], 0.0).then_inc(S["ones_row"], 1)
                        dve.memset(m3[0:n, u, :, :, 0:n], 0.0).then_inc(S["ones_row"], 1)
                        dve.wait_ge(S["ones_row"], done(5))
                    for h in range(H):
                        if h == 2 and two:
                            dve.wait_ge(S["u"], done(q))
                            dve.tensor_copy(parity(xu[:, 1]), odd_even(pD)).then_inc(S["us"], 1)
                        if h == 10 and two:
                            norm_mean(dve, q, n2, pD, True)
                        dve.wait_ge(S["ah"], done(H * t + h))
                        dve.memset(pace[:, h:h + 1], 0.0)
                        pv = (pA, pA, pB, pB)[h % 4][0:n, h % 2].rearrange("p (w t) -> p w t", w=4)[:, :, 0:n]
                        dve.copy_predicated(lT[0:n, h, 0:n], mask[0:n, 0, 0:n], pv[:, 0])
                        dve.copy_predicated(m3[0:n, u, h, :, 0:n], mask[0:n, 1:4, 0:n], pv[:, 1:4]).then_inc(S["am"], 1)
                        if h % 4 == 3:
                            g, hs = h // 4, slice(h - 3, h + 1)
                            dve.wait_ge(S["am"], done(H * t + h))
                            idb = ident[0:n, None, 0:n].broadcast_to([n, 4, n])
                            dve.tensor_tensor(ph[0:n, hs, 0:n], lT[0:n, hs, 0:n], idb, ALU.add).then_inc(S["pht"], 1)
                            dve.wait_ge(S["pht"], done(3 * t + g))
                            w1b = w1[0:n, None, 0:n].broadcast_to([n, 4, n])
                            dve.tensor_tensor(tt16[0:n, hs, 0:n], ph[0:n, hs, 0:n], w1b, ALU.mult).then_inc(S["t2t"], 1)
                if two:
                    dve.wait_ge(S["ds"], done(q))
                    dve.tensor_tensor(st[:], sc[:], pD[:, 0, 0:RB * HD].rearrange("p (b d) -> p b d", b=RB), ALU.add).then_inc(S["dsa"], 1)
                    dve.wait_ge(S["dsa"], done(q))
                    dve.tensor_tensor(st[:], st[:], ep[:, u2, :, P:P + 1].broadcast_to([P, RB, HD]), ALU.mult).then_inc(S["sn"], 1)
                    norm_var(dve, q, n2)
                if has1(t):
                    dve.wait_ge(S["bonus"], done(t))
                    dve.tensor_copy(bon[0:n, u], pC[0:n, 0, 0:H]).then_inc(S["bonc"], 1)
                    for l in levels(n):
                        for g in range(3):
                            hs = slice(4 * g, 4 * g + 4)
                            lb = lvl[0:n, l, None, 0:n].broadcast_to([n, 4, n])
                            dve.wait_ge(S["p1"], done(lix(t, l, g)))
                            dve.tensor_tensor(x16[0:n, hs, 0:n], bank(pB, g % 2, n), lb, ALU.mult).then_inc(S["xm"], 1)
                        if has2(t):
                            meanwhile(dve, q, n2, l, n)
                    if n == P:
                        key_scaled(dve, t + 1)
                    for g in range(3):
                        hs = slice(4 * g, 4 * g + 4)
                        idb = ident[0:n, None, 0:n].broadcast_to([n, 4, n])
                        dve.wait_ge(S["nr"], done(3 * t + g))
                        dve.tensor_tensor(x16[0:n, hs, 0:n], bank(pB, g % 2, n), idb, ALU.add).then_inc(S["rr"], 1)
                    for g in range(3):
                        hs = slice(4 * g, 4 * g + 4)
                        dve.wait_ge(S["nt"], done(3 * t + g))
                        dve.tensor_tensor(tt[0:n, u, hs, 0:n], tt16[0:n, hs, 0:n], bank(pC, g % 2, n), ALU.add).then_inc(S["ttf"], 1)
                else:
                    decode(dve)
                    norm_mean(dve, q, n2, None, False)
                    norm_var(dve, q, n2)
                    norm_apply(dve, q, n2)
                    gate_apply(dve, q, n2)
                    finish(dve, q, n2)
                dve.drain().then_inc(turn["dve"], 1)

            def key_scaled(dve, t):
                dve.wait_ge(S["sq"], done(t - 1))
                dve.wait_ge(f_in, landed(t))
                dve.tensor_tensor(kn[:], fm[:, RB:2 * RB], bc(kk, P), ALU.mult).then_inc(S["kq"], 1)

            def meanwhile(dve, q, n2, l, n):
                if l == 0:
                    norm_apply(dve, q, n2)
                if l == (2 if n == P else 1):
                    gate_apply(dve, q, n2)
                if l == (4 if n == P else 1):
                    finish(dve, q, n2)

            def norm_mean(dve, q, n2, src, wait):
                if wait:
                    dve.wait_ge(S["o"], done(q))
                for c in range(2):
                    o = odd_even(src, n2)[:, c] if wait else parity(on, n2)[:, c]
                    ins = dve.tensor_reduce(mv[0:n2, 0, c::2], o, AX, ALU.add)
                ins.then_inc(S["mean"], 1)
                dve.wait_ge(S["mean"], done(q))
                dve.tensor_scalar(mv[0:n2, 1], mv[0:n2, 0], -1.0 / HD, None, ALU.mult).then_inc(S["nmean"], 1)
                dve.wait_ge(S["nmean"], done(q))
                for c in range(2):
                    o = odd_even(src, n2)[:, c] if wait else parity(on, n2)[:, c]
                    ins = dve.tensor_tensor(parity(oc, n2)[:, c], o,
                                            mv[0:n2, 1, c::2, None].broadcast_to([n2, 6, HD]), ALU.add)
                ins.then_inc(S["oc"], 1)

            def norm_var(dve, q, n2):
                dve.wait_ge(S["sqo"], done(q))
                dve.tensor_reduce(mv[0:n2, 2], heads(on, n2), AX, ALU.add).then_inc(S["var"], 1)

            def norm_apply(dve, q, n2):
                dve.wait_ge(S["rs"], done(q))
                dve.tensor_tensor(heads(on, n2), heads(oc, n2), mv[0:n2, 3, :, None].broadcast_to([n2, H, HD]), ALU.mult).then_inc(S["onr"], 1)

            def gate_apply(dve, q, n2):
                dve.wait_ge(S["onb"], done(q))
                dve.wait_ge(S["g"], done(q))
                dve.tensor_tensor(cut(on, n2), cut(on, n2), halves(pD, n2), ALU.mult).then_inc(S["og"], 1)

            def finish(dve, q, n2):
                dve.wait_ge(S["oh"], done(q))
                dve.wait_ge(S["plh"], done(q))
                for c in range(2):
                    ins = dve.tensor_tensor(oT[:, 3 * c:3 * c + 3, 1, 0:n2], pD[:, c, 0:384].rearrange("p (b t) -> p b t", b=3)[:, :, 0:n2],
                                            oT[:, 3 * c:3 * c + 3, 0, 0:n2].bitcast(F32), ALU.subtract)
                ins.then_inc(S["ol"], 1)
                for b in range(2):
                    ins = dve.scalar_tensor_tensor(oT[:, 6 + b, 1, 0:n2], pD[:, b, 384:384 + n2], pscale[:, b:b + 1],
                                                   oT[:, 6 + b, 0, 0:n2].bitcast(F32), ALU.mult, ALU.subtract)
                ins.then_inc(S["pll"], 1)

            def decode(dve):
                sb = sel[:, :, None].broadcast_to([TS, NSEQ, HD])
                for w in range(2):
                    for h in range(H):
                        j = w * H + h
                        dve.wait_ge(S["fs"], done(j))
                        t4 = tmp[:, j % 2].rearrange("p (s d) -> p s d", s=NSEQ)
                        dve.tensor_tensor(t4, (pA, pA, pB, pB)[j % 4][0:TS, j % 2].rearrange("p (s d) -> p s d", s=NSEQ), sb, ALU.mult).then_inc(S["fr"], 1)
                        dve.wait_ge(S["fr"], done(j))
                        dst = (xu[0:TS, 0] if w == 0 else on[0:TS])[:, h * HD:h * HD + HD]
                        dve.tensor_reduce(dst, tmp[:, j % 2].rearrange("p (s d) -> p d s", s=NSEQ), AX, ALU.add).then_inc(S["fx"], 1)
                dve.wait_ge(S["fx"], done(2 * H - 1))
                dve.wait_ge(S["x"], done(NT))
                dve.tensor_tensor(parity(xu[:, 0], TS), parity(xu[:, 0], TS), odd_even(pD, TS), ALU.add).then_inc(S["xs"], 1)
                dve.wait_ge(S["u"], done(NT))
                dve.tensor_copy(parity(xu[:, 1], TS), odd_even(pC, TS)).then_inc(S["us"], 1)
                dve.wait_ge(S["o"], done(NT))
                dve.wait_ge(S["us"], done(NT))
                dve.tensor_tensor(parity(on, TS), parity(on, TS), odd_even(pD, TS), ALU.add).then_inc(S["fo"], 1)
                for h in range(H + 1):
                    if h < H:
                        if h >= 2:
                            dve.wait_ge(S["fu"], done(h - 2))
                        for w, src in ((0, xu[0:TS, 1]), (1, vt[0:TS, 0])):
                            t4 = spread[h % 2][w].rearrange("p (s d) -> p s d", s=NSEQ)
                            dve.tensor_tensor(t4, src[:, None, h * HD:h * HD + HD].broadcast_to([TS, NSEQ, HD]), sb, ALU.mult).then_inc(S["fda"], 1)
                    if h and h % 2 == 0:
                        b = h // 2 - 1
                        dve.wait_ge(S["fu"], done(h - 1))
                        sv = sS[:, b].rearrange("p s d -> p (s d)")
                        dve.tensor_tensor(sv, sv, pB[:, b % 2], ALU.add).then_inc(S["dsa"], 1)
                        dve.wait_ge(S["dsa"], done(NT + b))
                        g8 = ep[:, 0, b, 0:NSEQ * (LSEQ + 1)].rearrange("p (s l) -> p s l", s=NSEQ)[:, :, LSEQ:LSEQ + 1]
                        dve.tensor_tensor(sS[:, b], sS[:, b], g8.broadcast_to([P, NSEQ, HD]), ALU.mult).then_inc(S["sS"], 1)
                dve.wait_ge(S["fo"], done(0))
            turns(dve, body)


        @block.tensor
        def _(pe):
            pe.wait_ge(cons, landed(NCONST - 1))
            pe.wait_ge(S["ones_row"], done(3))
            pe.wait_ge(S["hb"], done(2))
            q_ = lambda h: slice(64 * (h % 2), 64 * (h % 2) + 64)
            hc = lambda h: slice(h * HD, h * HD + HD)

            def pdh(p, h, n):
                return p[0:n, h % 2, (h // 2) * HD:(h // 2) * HD + HD]

            def turn6(dst_of, src_of, n, sem, tok_out):
                for b in range(RB):
                    ins = pe.transpose(dst_of(b), src_of(b), ident[:] if tok_out else ident[0:n, 0:n])
                ins.then_inc(S[sem], 1)

            def body(t, u, n):
                if has1(t):
                    pe.wait_ge(S["am"], done(H * t - 1))
                    pe.wait_ge(S["sq"], done(t))
                    for b in range(RB):
                        mm = pe.matmul(pA[0:n, 0, 384 + 2 * b:386 + 2 * b], sq[:, b, 0:n], hsel[:], start=True, stop=True)
                    mm.then_inc(S["ss"], 1)
                    pe.wait_ge(S["tw"], done(t))
                    for c in range(2):
                        mm = pe.matmul(pA[0:n, c, 0:384], tw[:, 0:n], wdec[:, 384 * c:384 * c + 384], start=True, stop=True)
                    mm.then_inc(S["z"], 1)
                    pe.wait_ge(S["rr"], done(3 * t - 1))
                    pe.wait_ge(f_in, landed(t))
                    for b in range(RB):
                        mm = pe.matmul(blk(pB, b, n), wiclr[64:P, b * P:b * P + P], fm[64:P, 18, 0:n], start=True, stop=True)
                    mm.then_inc(S["a"], 1)
                    pe.wait_ge(S["ld"], done(t))
                    wd = P + 1 if n == P else NSEQ * (LSEQ + 1)
                    for b in range(RB):
                        mm = pe.matmul(blk(pA, b, wd, P + 1), ld[0:n, b * P:b * P + P], (trip if n == P else tris)[0:n, 0:wd], start=True, stop=True)
                    mm.then_inc(S["c"], 1)
                begin(pe, "pe", t)
                q, u2, n2 = t - 1, 1 - u, size2(t)
                two = has2(t) and n2 == P
                if has1(t):
                    pe.wait_ge(S["tha"], done(t))
                    turn6(lambda b: blk(pB, b, P, P, n), lambda b: fm[:, 2 * RB + b, 0:n], n, "vt", True)
                if two:
                    pe.wait_ge(S["s0c"], done(q))
                    inner(u2, range(0, 6))
                if has1(t):
                    pe.wait_ge(S["rb"], done(t))
                    turn6(lambda b: blk(pC, b, n), lambda b: be[:].rearrange("p b t -> p (b t)")[0:n, b * P:b * P + P], n, "rt", False)
                    pe.wait_ge(S["vts"], done(t))
                    pe.wait_ge(S["ke"], done(t))
                    turn6(lambda b: blk(pB, b, P, P, n), lambda b: ke[:, b, 0:n], n, "ket", True)
                if two:
                    inner(u2, range(6, H))
                if has1(t):
                    pe.wait_ge(S["be"], done(t))
                    turn6(lambda b: blk(pC, b, P, P, n), lambda b: be[:, b, 0:n], n, "bet", True)
                    pe.wait_ge(S["al"], done(t))
                    pe.wait_ge(S["re"], done(t))
                    pe.wait_ge(S["em"], done(t))
                    for h in range(H):
                        if h == 2:
                            if two:
                                pe.wait_ge(S["xs"], done(q))
                                for k in range(H):
                                    mm = pe.matmul(pdh(pD, k, n2), tt[:, u2, k], xu[:, 0, hc(k)], start=True, stop=True)
                                mm.then_inc(S["u"], 1)
                            pe.wait_ge(S["kets"], done(t))
                        if two and 4 <= h < 10:
                            pe.wait_ge(S["us"], done(q))
                            outputs(u2, range(2 * h - 8, 2 * h - 6))
                        if h >= 4:
                            pe.wait_ge(S["am"], done(H * t + h - 4))
                        o = (pA, pA, pB, pB)[h % 4][0:n, h % 2].rearrange("p (w a t) -> p w a t", w=2, a=2)
                        pe.matmul(o[:, 0, :, 0:n], be[q_(h), h // 2, 0:n], ar[q_(h), u, h // 2, :, 0:n], start=True, stop=True)
                        mm = pe.matmul(o[:, 1, :, 0:n], ke[q_(h), h // 2, 0:n], ar[q_(h), u, h // 2, :, 0:n], start=True, stop=True)
                        mm.then_inc(S["ah"], 1)
                    pe.wait_ge(S["bets"], done(t))
                    pe.wait_ge(S["rkp"], done(t))
                    for b in range(RB):
                        mm = pe.matmul(pC[0:n, 0, 2 * b:2 * b + 2], sq[:, b, 0:n], rk[:, b], start=True, stop=True)
                    mm.then_inc(S["bonus"], 1)
                if two:
                    states(q, u2)
                if has1(t):
                    pe.wait_ge(S["am"], done(H * t + H - 1))
                    for g in range(3):
                        pe.wait_ge(S["t2t"], done(3 * t + g))
                        if g == 2:
                            pe.wait_ge(S["t2s"], done(3 * t))
                        for h in range(4):
                            mm = pe.transpose(bank16(g, n)[:, h], tt16[0:n, 4 * g + h, 0:n], ident16[0:n, 0:n])
                        mm.then_inc(S["t2"], 1)
                    pe.wait_ge(S["t2s"], done(3 * t + 2))
                    for g in range(3):
                        if g == 2:
                            pe.wait_ge(S["xm"], done(lix(t, 0, 0)))
                        first_product(t, 0, g, n)
                    pe.wait_ge(S["bonc"], done(t))
                    for l in levels(n):
                        for g in range(3):
                            pe.wait_ge(S["xm"], done(lix(t, l, g)))
                            if g or l:
                                pe.wait_ge(S["tc"], done(lix(t, l, g - 1) if g else lix(t, l - 1, 2)))
                            for h in range(4):
                                k = 4 * g + h
                                mm = pe.matmul(bank(pC, 0, n)[:, h], tt16[0:n, k, 0:n], x16[0:n, k, 0:n], start=True, stop=True)
                            mm.then_inc(S["tp"], 1)
                            if g or l:
                                pe.wait_ge(S["ttc"], done(lix(t, l, g - 1) if g else lix(t, l - 1, 2)))
                            for h in range(4):
                                k = 4 * g + h
                                mm = pe.matmul(bank(pC, 1, n)[:, h], x16[0:n, k, 0:n], tt16[0:n, k, 0:n], start=True, stop=True)
                            mm.then_inc(S["tpt"], 1)
                            if g:
                                pe.wait_ge(S["xm"], done(lix(t, l, 2 if g == 1 else 1)))
                                if l != levels(n)[-1]:
                                    first_product(t, l + 1, g - 1, n)
                                else:
                                    residual(t, g - 1, n)
                            if has2(t):
                                meanwhile(t, q, u2, n2, l, g, n)
                        if l != levels(n)[-1]:
                            pe.wait_ge(S["tc"], done(lix(t, l, 2)))
                            pe.wait_ge(S["xm"], done(lix(t, l + 1, 0)))
                            first_product(t, l + 1, 2, n)
                    pe.wait_ge(S["ttc"], done(lix(t, levels(n)[-1], 2)))
                    pe.wait_ge(S["rr"], done(3 * t))
                    residual(t, 2, n)
                    for g in range(3):
                        pe.wait_ge(S["rr"], done(3 * t + g))
                        if g == 2:
                            pe.wait_ge(S["ttf"], done(3 * t))
                        for h in range(4):
                            k = 4 * g + h
                            mm = pe.matmul(bank(pC, g % 2, n)[:, h], x16[0:n, k, 0:n], tt16[0:n, k, 0:n], start=True, stop=True)
                        mm.then_inc(S["nt"], 1)
                else:
                    decode(u2)
                    gate(t, q, u2, n2)
                    mixed(t, q, u2, n2)
                pe.drain().then_inc(turn["pe"], 1)

            def first_product(t, l, g, n):
                for h in range(4):
                    mm = pe.matmul(bank(pB, g % 2, n)[:, h], ph[0:n, 4 * g + h, 0:n], t16[0:n, 4 * g + h, 0:n], start=True, stop=True)
                mm.then_inc(S["p1"], 1)

            def residual(t, g, n):
                pe.wait_ge(S["plt"], done(3 * t + g))
                for h in range(4):
                    k, o = 4 * g + h, bank(pB, g % 2, n)[:, h]
                    pe.matmul(o, nident16[0:n, 0:n], t16[0:n, k, 0:n], start=True, stop=False)
                    pe.matmul(o, ph[0:n, k, 0:n], t16[0:n, k, 0:n], start=False, stop=False)
                    mm = pe.matmul(o, pl[0:n, k, 0:n], t16[0:n, k, 0:n], start=False, stop=True)
                mm.then_inc(S["nr"], 1)

            def inner(u2, hs):
                for h in hs:
                    pe.matmul(pdh(pD, h, P), ar[q_(h), u2, h // 2, 0], sc[q_(h), h // 2], start=True, stop=False)
                    mm = pe.matmul(pdh(pD, h, P), m3[:, u2, h, 1], vt[:, u2, hc(h)], start=False, stop=True)
                    if h == H - 1:
                        mm.then_inc(S["x"], 1)

            def outputs(u2, hs):
                for h in hs:
                    o = pdh(pD, h, P)
                    pe.matmul(o, ar[q_(h), u2, h // 2, 1], sc[q_(h), h // 2], start=True, stop=False)
                    pe.matmul(o, m3[:, u2, h, 0], xu[:, 1, hc(h)], start=False, stop=False)
                    mm = pe.matmul(o, m3[:, u2, h, 2], vt[:, u2, hc(h)], start=False, stop=True)
                    if h == H - 1:
                        mm.then_inc(S["o"], 1)

            def states(q, u2):
                pe.wait_ge(S["oc"], done(q))
                for h in range(H):
                    o = pD[q_(h), 0, (h // 2) * HD:(h // 2) * HD + HD]
                    pe.matmul(o, bet[:, u2, hc(h)], xu[:, 1, hc(h)], start=True, stop=False)
                    mm = pe.matmul(o, ket[:, u2, hc(h)], vt[:, u2, hc(h)], start=False, stop=True)
                mm.then_inc(S["ds"], 1)

            def meanwhile(t, q, u2, n2, l, g, n):
                if (l, g) == (0, 1):
                    gate(t, q, u2, n2)
                if (l, g) == ((3, 1) if n == P else (1, 2)):
                    mixed(t, q, u2, n2)

            def gate(t, q, u2, n2):
                if not isinstance(q, int) or q < NT:
                    pe.wait_ge(S["sn"], done(q))
                pe.wait_ge(S["sgm"], done(q))
                for c in range(2):
                    mm = pe.matmul(pD[0:n2, c, 0:384], sg[:, u2, 0:n2], wgate[:, 384 * c:384 * c + 384], start=True, stop=True)
                mm.then_inc(S["g"], 1)

            def mixed(t, q, u2, n2):
                pe.wait_ge(S["og"], done(q))
                turn6(lambda b: blk(pD, b, n2), lambda b: on[0:n2, b * P:b * P + P], n2, "ot", False)
                pe.wait_ge(S["fd"], done(2 * q + 1))
                for b in range(2):
                    mm = pe.matmul(pD[:, b, 384:384 + n2], pmap[:, b], pc[:, b, 0:n2], start=True, stop=True)
                mm.then_inc(S["pmm"], 1)

            def decode(u2):
                n = TS
                pe.wait_ge(st_in, landed(0))
                for h in range(H):
                    mm = pe.matmul(pdh(pD, h, n), m3[0:n, 0, h, 1, 0:n], vt[0:n, 0, hc(h)], start=True, stop=True)
                mm.then_inc(S["x"], 1)
                for w in range(2):
                    for h in range(H):
                        j = w * H + h
                        if j >= 4:
                            pe.wait_ge(S["fr"], done(j - 4))
                        rhs = sS[q_(h), h // 2].rearrange("p s d -> p (s d)")
                        pe.matmul((pA, pA, pB, pB)[j % 4][0:n, j % 2], ar[q_(h), 0, h // 2, w, 0:n], rhs, start=True, stop=True).then_inc(S["fs"], 1)
                pe.wait_ge(S["xs"], done(NT))
                for h in range(H):
                    mm = pe.matmul(pdh(pC, h, n), tt[0:n, 0, h, 0:n], xu[0:n, 0, hc(h)], start=True, stop=True)
                mm.then_inc(S["u"], 1)
                pe.wait_ge(S["us"], done(NT))
                for h in range(H):
                    o = pdh(pD, h, n)
                    pe.matmul(o, m3[0:n, 0, h, 0, 0:n], xu[0:n, 1, hc(h)], start=True, stop=False)
                    mm = pe.matmul(o, m3[0:n, 0, h, 2, 0:n], vt[0:n, 0, hc(h)], start=False, stop=True)
                mm.then_inc(S["o"], 1)
                for h in range(H):
                    pe.wait_ge(S["fda"], done(2 * h + 1))
                    if h % 2 == 0 and h >= 4:
                        pe.wait_ge(S["sS"], done(h // 2 - 2))
                    o = pB[q_(h), (h // 2) % 2]
                    pe.matmul(o, bet[0:n, 0, hc(h)], spread[h % 2][0], start=True, stop=False)
                    pe.matmul(o, ket[0:n, 0, hc(h)], spread[h % 2][1], start=False, stop=True).then_inc(S["fu"], 1)
                pe.wait_ge(S["fo"], done(0))
            turns(pe, body)



def phase_c(nc, io, dr):
    with ExitStack() as ctx:
        m = Scope(nc, ctx, "c")
        wh = m.sb("wh", [P, 2 * KB, D], F32R)
        wl = m.sb("wl", [P, 2 * KB, D], F32R)
        o = m.sb("o", [P, 2, KB, 2, P], F32R)
        gate = m.sb("gate", [P, 2, 2 * D])
        mT = m.sb("mT", [P, KB, 2, P], F32R)
        x = m.sb("x", [P, 2, D])
        yn = m.sb("yn", [P, D])
        h = m.sb("h", [P, D])
        hT = m.sb("hT", [P, 2, KB, 2, P], F32R)
        gpost = m.sb("gpost", [P, D])
        ident = m.sb("ident", [P, P])
        stat = m.sb("stat", [P, 8])
        mhalf, eps = m.sb("mhalf", [P, 1]), m.sb("eps", [P, 1])
        pa = m.ps("pa", [P, 2, 512])
        pb = m.ps("pb", [P, 2, 512])
        py = m.ps("py", [P, 2, 512])
        pt = m.ps("pt", [P, KB, P])
        flat = lambda t: t[:].rearrange("p a b -> p (a b)")

        cons = m.sem("consts", 16)
        w_in = [m.sem(f"w_in{u}", 16) for u in range(2)]
        wh_done, wl_done = m.sem("wh_done"), m.sem("wl_done")
        o_in = [m.sem(f"o_in{u}", 16) for u in range(2)]
        g_in = [m.sem(f"g_in{u}", 16) for u in range(2)]
        x_in = [m.sem(f"x_in{u}", 16) for u in range(2)]
        branch_done, gated_a, gated_b, merged_done = (m.sem(n) for n in ("branch_done", "gated_a", "gated_b", "merged_done"))
        tm_done, mh_done, ml_done, y_done = (m.sem(n) for n in ("tm_done", "mh_done", "ml_done", "y_done"))
        ss_done, var_done, r_done, yn_done, x1_done = (m.sem(n) for n in ("ss_done", "var_done", "r_done", "yn_done", "x1_done"))
        ss2_done, var2_done, r2_done, h_done = (m.sem(n) for n in ("ss2_done", "var2_done", "r2_done", "h_done"))
        th_done, hh_done, hl_done = m.sem("th_done"), m.sem("hh_done"), m.sem("hl_done")
        x1_st = [m.sem(f"x1_stored{u}", 16) for u in range(2)]
        h_st = [m.sem(f"h_stored{u}", 16) for u in range(2)]
        mhalf_set = m.sem("mhalf_set")
        block = m.start()
        size = lambda t: TS if isinstance(t, int) and t == NT else P
        rows = lambda t, n: slice(t * P, t * P + n) if isinstance(t, int) else bass.ds(t * P, n)

        def tiles(eng, body, first=0):
            body(0, 0, 0)
            with eng.Fori(0, 7) as i:
                body(2 * i + 1, 1, i)
                body(2 * i + 2, 0, i + 1)
            body(15, 1, 7)
            body(16, 0, 8)

        @block.sync
        def _(sp):
            sp.dma_start(gpost[:], io["gpost"]).then_inc(cons, 16)
            sp.dma_start(ident[:], io["ident"]).then_inc(cons, 16)
            for c in range(KB):
                sp.wait_ge(wl_done, done(c - 2))
                if c == 4:
                    for u in range(2):
                        sp.dma_start(o[:, u].bitcast(F32), dr["o"][u]).then_inc(o_in[u], 16)
                w = io["w_branch"] if c < 4 else io["w_out"]
                r = (c % 4) * 2 * P
                sp.dma_start(gate[:, c % 2].rearrange("p (k n) -> p k n", k=2),
                             w[r:r + 2 * P].rearrange("(k p) n -> p k n", p=P)).then_inc(w_in[c % 2], 16)
            sp.wait_ge(wl_done, done(KB - 1))

            def store_h(t, u):
                n = size(t)
                sp.wait_ge(hl_done, done(t))
                sp.dma_start(dr["h"][t, :, :, :, 0:n], hT[:, u, :, :, 0:n].bitcast(F32)).then_inc(h_st[u], 16)

            def store_x1(t, u):
                n = size(t)
                sp.wait_ge(x1_done, done(t))
                sp.dma_start(dr["x1"][rows(t, n)], x[0:n, u]).then_inc(x1_st[u], 16)

            def step(t, u, i):
                n = size(t)
                if not isinstance(t, int) or t > 1:
                    sp.wait_ge(branch_done, done(t - 2))
                    sp.dma_start(o[:, u, :, :, 0:n].bitcast(F32), dr["o"][t, :, :, :, 0:n]).then_inc(o_in[u], 16)
                sp.wait_ge(tm_done, done(t - 2))
                sp.dma_start(gate[0:n, u], dr["gate"][rows(t, n)]).then_inc(g_in[u], 16)
                if not isinstance(t, int) or t >= 3:
                    store_h(t - 3, 1 - u)
                if not isinstance(t, int) or t >= 2:
                    store_x1(t - 2, u)
                sp.wait_ge(x1_st[u], landed(i - 1))
                sp.wait_ge(h_done, done(t - 2))
                sp.dma_start(x[0:n, u], io["x"][rows(t, n)]).then_inc(x_in[u], 16)
            for t in range(3):
                step(t, t % 2, t // 2)
            with sp.Fori(1, 7) as i:
                step(2 * i + 1, 1, i)
                step(2 * i + 2, 0, i + 1)
            step(15, 1, 7)
            step(16, 0, 8)
            store_h(14, 0)
            store_x1(15, 1)
            store_h(15, 1)
            store_x1(16, 0)
            store_h(16, 0)
            for u, last in ((0, 8), (1, 7)):
                sp.wait_ge(x1_st[u], landed(last))
                sp.wait_ge(h_st[u], landed(last))

        @block.gpsimd
        def _(pool):
            pool.memset(mhalf[:], -0.5).then_inc(mhalf_set, 1)
            pool.memset(eps[:], EPS).then_inc(mhalf_set, 1)
            pool.wait_ge(mhalf_set, done(1))

            def norms(t, u, i):
                n = size(t)
                pool.wait_ge(ss_done, done(t))
                pool.tensor_tensor(stat[0:n, 1:2], stat[0:n, 0:1], eps[0:n], ALU.add).then_inc(var_done, 1)
                pool.wait_ge(yn_done, done(t - 1))
                pool.wait_ge(var_done, done(t))
                pool.tensor_tensor(stat[0:n, 2:3], stat[0:n, 1:2], mhalf[0:n], ALU.pow).then_inc(r_done, 1)
                pool.wait_ge(ss2_done, done(t))
                pool.tensor_tensor(stat[0:n, 4:5], stat[0:n, 3:4], eps[0:n], ALU.add).then_inc(var2_done, 1)
                pool.wait_ge(h_done, done(t - 1))
                pool.wait_ge(var2_done, done(t))
                pool.tensor_tensor(stat[0:n, 5:6], stat[0:n, 4:5], mhalf[0:n], ALU.pow).then_inc(r2_done, 1)
            tiles(pool, norms)

        @block.scalar
        def _(act):
            for c in range(KB):
                act.wait_ge(w_in[c % 2], landed(c // 2))
                act.activation(wh[:, 2 * c:2 * c + 2], gate[:, c % 2].rearrange("p (k n) -> p k n", k=2), ACT.Copy).then_inc(wh_done, 1)

            def stage(t, u, i):
                n = size(t)
                act.wait_ge(y_done, done(t - 1))
                act.wait_ge(tm_done, done(t))
                act.activation(mT[:, :, 0, 0:n], pt[:, :, 0:n], ACT.Copy).then_inc(mh_done, 1)

            def norm(t, u, i):
                n = size(t)
                act.wait_ge(x1_done, done(t - 1))
                act.wait_ge(y_done, done(t))
                act.activation(yn[0:n], flat(py)[0:n], ACT.Square, scale=D ** -0.5, accum_out=stat[0:n, 0:1]).then_inc(ss_done, 1)
                act.wait_ge(th_done, done(t - 1))
                act.wait_ge(x1_done, done(t))
                act.activation(h[0:n], x[0:n, u], ACT.Square, scale=D ** -0.5, accum_out=stat[0:n, 3:4]).then_inc(ss2_done, 1)
                act.wait_ge(r2_done, done(t))
                act.activation(h[0:n], x[0:n, u], ACT.Copy, scale=stat[0:n, 5:6]).then_inc(h_done, 1)
                act.wait_ge(h_st[u], landed(i - 1))
                act.wait_ge(th_done, done(t))
                act.activation(hT[:, u, :, 0, 0:n], pt[:, :, 0:n], ACT.Copy).then_inc(hh_done, 1)
            stage(0, 0, 0)
            with act.Fori(0, 7) as i:
                stage(2 * i + 1, 1, i)
                norm(2 * i, 0, i)
                stage(2 * i + 2, 0, i + 1)
                norm(2 * i + 1, 1, i)
            stage(15, 1, 7)
            norm(14, 0, 7)
            stage(16, 0, 8)
            norm(15, 1, 7)
            norm(16, 0, 8)

        @block.vector
        def _(dve):
            for c in range(KB):
                dve.wait_ge(wh_done, done(c))
                dve.tensor_tensor(wl[:, 2 * c:2 * c + 2], gate[:, c % 2].rearrange("p (k n) -> p k n", k=2),
                                  wh[:, 2 * c:2 * c + 2].bitcast(F32), ALU.subtract).then_inc(wl_done, 1)
            dve.wait_ge(cons, landed(1))

            def merge(t, u, i):
                n = size(t)
                dve.wait_ge(g_in[u], landed(i))
                dve.wait_ge(branch_done, done(t))
                dve.tensor_tensor(gate[0:n, u, 0:D], gate[0:n, u, 0:D], flat(pa)[0:n], ALU.mult).then_inc(gated_a, 1)
                dve.tensor_tensor(gate[0:n, u, D:], gate[0:n, u, D:], flat(pb)[0:n], ALU.mult).then_inc(gated_b, 1)
                dve.wait_ge(gated_a, done(t))
                dve.wait_ge(gated_b, done(t))
                dve.tensor_tensor(gate[0:n, u, 0:D], gate[0:n, u, 0:D], gate[0:n, u, D:], ALU.add).then_inc(merged_done, 1)

            def stage(t, u, i):
                n = size(t)
                dve.wait_ge(mh_done, done(t))
                dve.tensor_tensor(mT[:, :, 1, 0:n], pt[:, :, 0:n], mT[:, :, 0, 0:n].bitcast(F32), ALU.subtract).then_inc(ml_done, 1)

            def norm(t, u, i):
                n = size(t)
                dve.wait_ge(r_done, done(t))
                dve.scalar_tensor_tensor(yn[0:n], flat(py)[0:n], stat[0:n, 2:3], gpost[0:n], ALU.mult, ALU.mult).then_inc(yn_done, 1)
                dve.wait_ge(x_in[u], landed(i))
                dve.wait_ge(yn_done, done(t))
                dve.tensor_tensor(x[0:n, u], x[0:n, u], yn[0:n], ALU.add).then_inc(x1_done, 1)

            def split(t, u, i):
                n = size(t)
                dve.wait_ge(hh_done, done(t))
                dve.tensor_tensor(hT[:, u, :, 1, 0:n], pt[:, :, 0:n], hT[:, u, :, 0, 0:n].bitcast(F32), ALU.subtract).then_inc(hl_done, 1)
            merge(0, 0, 0)
            stage(0, 0, 0)
            merge(1, 1, 0)
            with dve.Fori(0, 7) as i:
                stage(2 * i + 1, 1, i)
                norm(2 * i, 0, i)
                merge(2 * i + 2, 0, i + 1)
                split(2 * i, 0, i)
                stage(2 * i + 2, 0, i + 1)
                norm(2 * i + 1, 1, i)
                merge(2 * i + 3, 1, i + 1)
                split(2 * i + 1, 1, i)
            stage(15, 1, 7)
            norm(14, 0, 7)
            merge(16, 0, 8)
            split(14, 0, 7)
            stage(16, 0, 8)
            norm(15, 1, 7)
            split(15, 1, 7)
            norm(16, 0, 8)
            split(16, 0, 8)

        @block.tensor
        def _(pe):
            def branch(t, u, i):
                n = size(t)
                if isinstance(t, int) and t == 0:
                    pe.wait_ge(wl_done, done(3))
                pe.wait_ge(o_in[u], landed(i))
                pe.wait_ge(merged_done, done(t - 1))
                for out, ks in ((pa, range(RB)), (pb, range(RB, KB))):
                    for c in range(2):
                        cols = slice(512 * c, 512 * c + 512)
                        for k in ks:
                            mm = split3(pe, out[0:n, c], (o[:, u, k, 0, 0:n], o[:, u, k, 1, 0:n]),
                                        (wh[:, k, cols], wl[:, k, cols]), k == ks[0], k == ks[-1])
                mm.then_inc(branch_done, 1)

            def turn_m(t, u, i):
                n = size(t)
                pe.wait_ge(hl_done, done(t - 2))
                pe.wait_ge(merged_done, done(t))
                for k in range(KB):
                    mm = pe.transpose(pt[:, k, 0:n], gate[0:n, u, k * P:k * P + P], ident[0:n, 0:n])
                mm.then_inc(tm_done, 1)

            def turn_h(t, u, i):
                n = size(t)
                if not (isinstance(t, int) and t == NT):
                    pe.wait_ge(ml_done, done(t + 1))
                pe.wait_ge(h_done, done(t))
                for k in range(KB):
                    mm = pe.transpose(pt[:, k, 0:n], h[0:n, k * P:k * P + P], ident[0:n, 0:n])
                mm.then_inc(th_done, 1)

            def project(t, u, i):
                n = size(t)
                pe.wait_ge(yn_done, done(t - 1))
                pe.wait_ge(ml_done, done(t))
                for c in range(2):
                    cols = slice(512 * c, 512 * c + 512)
                    for k in range(KB):
                        mm = split3(pe, py[0:n, c], (mT[:, k, 0, 0:n], mT[:, k, 1, 0:n]),
                                    (wh[:, KB + k, cols], wl[:, KB + k, cols]), k == 0, k == KB - 1)
                mm.then_inc(y_done, 1)
            pe.wait_ge(cons, landed(1))
            branch(0, 0, 0)
            turn_m(0, 0, 0)
            branch(1, 1, 0)
            pe.wait_ge(wl_done, done(KB - 1))
            project(0, 0, 0)
            with pe.Fori(0, 7) as i:
                turn_m(2 * i + 1, 1, i)
                branch(2 * i + 2, 0, i + 1)
                turn_h(2 * i, 0, i)
                project(2 * i + 1, 1, i)
                turn_m(2 * i + 2, 0, i + 1)
                branch(2 * i + 3, 1, i + 1)
                turn_h(2 * i + 1, 1, i)
                project(2 * i + 2, 0, i + 1)
            turn_m(15, 1, 7)
            branch(16, 0, 8)
            turn_h(14, 0, 7)
            project(15, 1, 7)
            turn_m(16, 0, 8)
            turn_h(15, 1, 7)
            project(16, 0, 8)
            turn_h(16, 0, 8)


def phase_d(nc, io, dr):
    with ExitStack() as ctx:
        m = Scope(nc, ctx, "d")
        hh = m.sb("hh", [P, KB, TT], F32R)
        hl = m.sb("hl", [P, KB, TT], F32R)
        wraw = m.sb("wraw", [P, 2, KB, WC])
        wh = m.sb("wh", [P, 2, KB, WC], F32R)
        wl = m.sb("wl", [P, 2, KB, WC], F32R)
        sg = m.sb("sg", [P, 2, 512])
        gu = m.sb("gu", [P, 2, 512])
        out = m.sb("out", [P, 2, 2, 512], F32R)
        gffn = m.sb("gffn", [P, KB])
        pg = m.ps("pg", [P, 2, 512])
        pu = m.ps("pu", [P, 2, 512])
        cons = m.sem("consts", 16)
        h_in = [m.sem(f"h_in{g}", 16) for g in range(5)]
        w_in = [m.sem(f"w_in{u}", 16) for u in range(2)]
        wg_done, wh_done, wl_done = m.sem("wg_done"), m.sem("wh_done"), m.sem("wl_done")
        g_done, u_done, silu_done, gu_done = (m.sem(n) for n in ("g_done", "u_done", "silu_done", "gu_done"))
        hi_done, lo_done = m.sem("hi_done"), m.sem("lo_done")
        stored = [m.sem(f"stored{u}", 16) for u in range(2)]
        block = m.start()
        groups = EVEN
        NG = len(groups)

        @block.sync
        def _(sp):
            sp.dma_start(gffn[:], io["gffnT"]).then_inc(cons, 16)
            for u in range(2):
                sp.dma_start(wraw[:, u], io["w_ffn_in"][u]).then_inc(w_in[u], 16)

            for q in range(NT + 1):
                n = P if q < NT else TS
                for part, dst in ((0, hh), (1, hl)):
                    sp.dma_start(dst[:, :, q * P:q * P + n].bitcast(F32), dr["h"][q, :, :, part, 0:n]).then_inc(h_in[q // 4], 16)

            def store(b, u, g):
                j = u * NG + g
                t0, n = groups[g]
                sp.wait_ge(lo_done, done(b * NG + g))
                for part in range(2):
                    sp.dma_start(dr["gu"][:, b, part, t0:t0 + n], out[:, j % 2, part, 0:n].bitcast(F32)).then_inc(stored[j % 2], 16)

            def load_w(b, u):
                sp.wait_ge(wl_done, done(b - 2))
                sp.dma_start(wraw[:, u], io["w_ffn_in"][b]).then_inc(w_in[u], 16)
            with sp.Fori(0, 10) as i:
                for u in range(2):
                    load_w(2 * i + u + 2, u)
                    for g in range(NG):
                        store(2 * i + u, u, g)
            for u in range(2):
                for g in range(NG):
                    store(20 + u, u, g)
            for s in range(2):
                sp.wait_ge(stored[s], landed(FB * NG - 1))

        @block.gpsimd
        def _(pool):
            pool.wait_ge(cons, landed(0))
            with pool.Fori(0, FB // 2) as i:
                for u in range(2):
                    pool.wait_ge(w_in[u], landed(i))
                    pool.tensor_tensor(wraw[:, u], wraw[:, u], gffn[:, :, None].broadcast_to([P, KB, WC]), ALU.mult).then_inc(wg_done, 1)

        @block.scalar
        def _(act):
            def hi_w(b, u):
                if not isinstance(b, int):
                    act.wait_ge(u_done, done((b - 1) * NG - 1))
                act.wait_ge(wg_done, done(b))
                act.activation(wh[:, u], wraw[:, u], ACT.Copy).then_inc(wh_done, 1)

            def job(i, u, g):
                j, n = (2 * i + u) * NG + g, groups[g][1]
                s = (u * NG + g) % 2
                act.wait_ge(gu_done, done(j - 2))
                act.wait_ge(g_done, done(j))
                act.activation(sg[:, s, 0:n], pg[:, s, 0:n], ACT.Silu).then_inc(silu_done, 1)
                act.wait_ge(stored[s], landed(2 * (i * NG + (u * NG + g) // 2) - 1))
                act.wait_ge(gu_done, done(j))
                act.activation(out[:, s, 0, 0:n], gu[:, s, 0:n], ACT.Copy).then_inc(hi_done, 1)

            hi_w(0, 0)
            hi_w(1, 1)
            with act.Fori(0, 10) as i:
                for u in range(2):
                    for g in range(NG):
                        job(i, u, g)
                    hi_w(2 * i + u + 2, u)
            for u in range(2):
                for g in range(NG):
                    job(10, u, g)

        @block.vector
        def _(dve):
            def lo_w(b, u):
                dve.wait_ge(wh_done, done(b))
                dve.tensor_tensor(wl[:, u], wraw[:, u], wh[:, u].bitcast(F32), ALU.subtract).then_inc(wl_done, 1)

            def job(b, u, g):
                j, n = b * NG + g, groups[g][1]
                s = (u * NG + g) % 2
                dve.wait_ge(u_done, done(j))
                dve.wait_ge(silu_done, done(j))
                dve.tensor_tensor(gu[:, s, 0:n], sg[:, s, 0:n], pu[:, s, 0:n], ALU.mult).then_inc(gu_done, 1)
                dve.wait_ge(hi_done, done(j))
                dve.tensor_tensor(out[:, s, 1, 0:n], gu[:, s, 0:n], out[:, s, 0, 0:n].bitcast(F32), ALU.subtract).then_inc(lo_done, 1)
            lo_w(0, 0)
            lo_w(1, 1)
            with dve.Fori(0, 10) as i:
                for u in range(2):
                    for g in range(NG):
                        job(2 * i + u, u, g)
                    lo_w(2 * i + u + 2, u)
            for u in range(2):
                for g in range(NG):
                    job(20 + u, u, g)

        @block.tensor
        def _(pe):
            def blockmm(b, u):
                pe.wait_ge(wl_done, done(b))
                for g, (t0, n) in enumerate(groups):
                    j, s, x = b * NG + g, (u * NG + g) % 2, slice(t0, t0 + n)
                    if isinstance(b, int) and b == 0:
                        pe.wait_ge(h_in[g], landed(7 if g < 4 else 1))
                    pe.wait_ge(gu_done, done(j - 2))
                    for half_, (acc, sem) in enumerate(((pg, g_done), (pu, u_done))):
                        w = slice(half_ * P, half_ * P + P)
                        for k in range(KB):
                            mm = split3(pe, acc[:, s, 0:n], (wh[:, u, k, w], wl[:, u, k, w]),
                                        (hh[:, k, x], hl[:, k, x]), k == 0, k == KB - 1)
                        mm.then_inc(sem, 1)
            blockmm(0, 0)
            blockmm(1, 1)
            with pe.Fori(1, 11) as i:
                for u in range(2):
                    blockmm(2 * i + u, u)


def phase_e(nc, io, dr):
    with ExitStack() as ctx:
        m = Scope(nc, ctx, "e")
        KH = FB // 2
        wh = m.sb("wh", [P, FB, D], F32R)
        wl = m.sb("wl", [P, FB, D], F32R)
        gu = m.sb("gu", [P, 2, KH, 2, P], F32R)
        x = m.sb("x", [P, 2, 512])
        gpost = m.sb("gpost", [P, D])
        stat = m.sb("stat", [P, 4])
        mhalf, eps = m.sb("mhalf", [P, 1]), m.sb("eps", [P, 1])
        py = m.ps("py", [P, 2, 2, 512])
        junk = m.ps("junk", [P, 2, 512])
        flat = lambda t: t.rearrange("p a b -> p (a b)")
        cons = m.sem("consts", 16)
        NW = 2 * FB
        w_in = [m.sem(f"w_in{c}", 16) for c in range(4)]
        stage = [x[:, 0], x[:, 1], gpost[:, 0:512], gpost[:, 512:D]]
        wh_done, wl_done = m.sem("wh_done"), m.sem("wl_done")
        gu_in = [m.sem(f"gu_in{u}", 16) for u in range(2)]
        half_done = [m.sem(f"half_done{u}") for u in range(2)]
        x_in, stored = m.sem("x_in", 16), m.sem("stored", 16)
        ss_done, var_done, r_done, yn_done, y_out = (m.sem(n) for n in ("ss_done", "var_done", "r_done", "yn_done", "y_out"))
        mhalf_set = m.sem("mhalf_set")
        block = m.start()
        size = lambda t: TS if isinstance(t, int) and t == NT else P
        rows = lambda t, n: slice(t * P, t * P + n) if isinstance(t, int) else bass.ds(t * P, n)

        @block.sync
        def _(sp):
            for c in range(NW):
                if c >= 4:
                    sp.wait_ge(wl_done, done(c - 4))
                sp.dma_start(stage[c % 4], io["w_ffn_out"][c // 2 * P:c // 2 * P + P, 512 * (c % 2):512 * (c % 2) + 512]).then_inc(w_in[c % 4], 16)
            sp.wait_ge(wl_done, done(NW - 1))
            sp.dma_start(gpost[:], io["gffnpost"]).then_inc(cons, 16)

            def tile_x(t):
                n = size(t)
                sp.wait_ge(stored, landed(t - 1))
                sp.dma_start(flat(x[0:n]), dr["x1"][rows(t, n)]).then_inc(x_in, 16)
                sp.wait_ge(y_out, done(t))
                sp.dma_start(io["o_y"][rows(t, n)], flat(x[0:n])).then_inc(stored, 16)
            with sp.Fori(0, NT) as t:
                tile_x(t)
            tile_x(NT)
            sp.wait_ge(stored, landed(NT))

        @block.gpsimd
        def _(pool):
            pool.memset(mhalf[:], -0.5).then_inc(mhalf_set, 1)
            pool.memset(eps[:], EPS).then_inc(mhalf_set, 1)
            pool.wait_ge(mhalf_set, done(1))

            def norm(t):
                n = size(t)
                pool.wait_ge(ss_done, done(t))
                pool.tensor_tensor(stat[0:n, 1:2], stat[0:n, 0:1], eps[0:n], ALU.add).then_inc(var_done, 1)
                pool.wait_ge(yn_done, done(t - 1))
                pool.wait_ge(var_done, done(t))
                pool.tensor_tensor(stat[0:n, 2:3], stat[0:n, 1:2], mhalf[0:n], ALU.pow).then_inc(r_done, 1)
            with pool.Fori(0, NT) as t:
                norm(t)
            norm(NT)

        @block.scalar
        def _(act):
            def load(t):
                n = size(t)
                for part in range(2):
                    act.wait_ge(half_done[part], done(t - 1))
                    act.dma_start(gu[:, part, :, :, 0:n].bitcast(F32), dr["gu"][:, part * KH:part * KH + KH, :, rows(t, n)]).then_inc(gu_in[part], 16)
            load(0)
            for c in range(NW):
                act.wait_ge(w_in[c % 4], landed(c // 4))
                act.activation(wh[:, c // 2, 512 * (c % 2):512 * (c % 2) + 512], stage[c % 4], ACT.Copy).then_inc(wh_done, 1)

            def square(t, u):
                n = size(t)
                act.wait_ge(yn_done, done(t - 1))
                act.wait_ge(half_done[1], done(t))
                act.activation(flat(junk[0:n]), flat(py[0:n, u]), ACT.Square, scale=D ** -0.5, accum_out=stat[0:n, 0:1]).then_inc(ss_done, 1)
            with act.Fori(0, NT // 2 - 1) as i:
                load(2 * i + 1)
                square(2 * i, 0)
                load(2 * i + 2)
                square(2 * i + 1, 1)
            load(15)
            square(14, 0)
            load(16)
            square(15, 1)
            square(NT, 0)

        @block.vector
        def _(dve):
            for c in range(NW):
                cols = slice(512 * (c % 2), 512 * (c % 2) + 512)
                dve.wait_ge(wh_done, done(c))
                dve.tensor_tensor(wl[:, c // 2, cols], stage[c % 4], wh[:, c // 2, cols].bitcast(F32), ALU.subtract).then_inc(wl_done, 1)
            dve.wait_ge(cons, landed(0))

            def norm(t, u):
                n = size(t)
                dve.wait_ge(r_done, done(t))
                dve.scalar_tensor_tensor(flat(py[0:n, u]), flat(py[0:n, u]), stat[0:n, 2:3], gpost[0:n], ALU.mult, ALU.mult).then_inc(yn_done, 1)
                dve.wait_ge(x_in, landed(t))
                dve.wait_ge(yn_done, done(t))
                dve.tensor_tensor(flat(x[0:n]), flat(x[0:n]), flat(py[0:n, u]), ALU.add).then_inc(y_out, 1)
            with dve.Fori(0, NT // 2) as i:
                norm(2 * i, 0)
                norm(2 * i + 1, 1)
            norm(NT, 0)

        @block.tensor
        def _(pe):
            def tile(t, u):
                n = size(t)
                pe.wait_ge(y_out, done(t - 2))
                for part in range(2):
                    pe.wait_ge(gu_in[part], landed(t))
                    first = isinstance(t, int) and t == 0
                    for c, k in ([(c, k) for k in range(KH) for c in range(2)] if first else [(c, k) for c in range(2) for k in range(KH)]):
                        cols, kk = slice(512 * c, 512 * c + 512), part * KH + k
                        if first and c == 0:
                            pe.wait_ge(wl_done, done(2 * kk + 1))
                        mm = split3(pe, py[0:n, u, c], (gu[:, part, k, 0, 0:n], gu[:, part, k, 1, 0:n]),
                                    (wh[:, kk, cols], wl[:, kk, cols]), kk == 0, kk == FB - 1)
                    mm.then_inc(half_done[part], 1)
            tile(0, 0)
            tile(1, 1)
            with pe.Fori(1, NT // 2) as i:
                tile(2 * i, 0)
                tile(2 * i + 1, 1)
            tile(NT, 0)




def program(nc, io, dr):
    for phase in (phase_a, phase_b, phase_c, phase_d, phase_e):
        phase(nc, io, dr)


SCRATCH = {
    "fm": [P, NFM, TT], "gate": [TT, 2 * D], "o": [NT + 1, P, KB, 2, P], "x1": [TT, D],
    "h": [NT + 1, P, KB, 2, P], "gu": [P, FB, 2, TT],
}
OUTPUTS = {
    "o_y": [TT, D], "o_shp": [P, NSH], "o_shs": [P, NSH, NSEQ], "o_wkvp": [P, RB, HD], "o_wkvs": [P, RB, NSEQ, HD],
    "o_poolp": [P, 2, HIST], "o_pools": [P, 2, NSEQ, HIST],
}


def build(nc, arrays):
    io = {n: nc.dram_tensor(f"in_{n}", a.shape, U32 if n.startswith("mask") else F32, kind="ExternalInput").ap() for n, a in arrays.items()}
    for n, shape in OUTPUTS.items():
        io[n] = nc.dram_tensor(n, shape, F32, kind="ExternalOutput").ap()
    dr = {n: nc.dram_tensor(f"s_{n}", shape, F32, kind="Internal").ap() for n, shape in SCRATCH.items()}
    program(nc, io, dr)


def lay_out(i):
    blocks = lambda v: np.ascontiguousarray(v.reshape(-1, P).T)
    rows = lambda v: np.ascontiguousarray(np.broadcast_to(v.reshape(1, -1), (P, v.size)))
    x = np.concatenate([i["x_prompt"].reshape(TP, D), i["x_sample"].reshape(TS, D)])
    xt = np.zeros((NT + 1, P, KB, P), x.dtype)
    for q in range(NT + 1):
        n = P if q < NT else TS
        xt[q, :, :, :n] = x[q * P:q * P + n].T.reshape(KB, P, n).transpose(1, 0, 2)
    wblk = lambda w: np.ascontiguousarray(w.reshape(KB, P, -1, WC).transpose(2, 1, 0, 3))
    wf = i["w_ffn_in"][0]
    wf = np.concatenate([wf[:, :FF].reshape(D, FB, P), wf[:, FF:].reshape(D, FB, P)], axis=2).reshape(D, -1)
    j = np.arange(P)
    t129 = np.arange(P + 1)
    trip = (j[:, None] < t129[None]).astype(np.float32) - (j[:, None] < P // 2).astype(np.float32)
    js = np.arange(TS)
    seg = np.arange(NSEQ * (LSEQ + 1))
    tris = ((js[:, None] // LSEQ == seg[None] // (LSEQ + 1)) & (js[:, None] % LSEQ < seg[None] % (LSEQ + 1))).astype(np.float32)
    s_, t_ = j[:, None], j[None]
    strict, incl = s_ < t_, s_ <= t_
    same = (s_ // LSEQ == t_ // LSEQ)
    lv = []
    for m in (2, 4, 8, 16, 32, 64):
        lv.append(((s_ // (2 * m) == t_ // (2 * m)) & (s_ % (2 * m) >= m) & (t_ % (2 * m) < m)) | (s_ == t_))
    w1 = (s_ == t_) | ((s_ // 2 == t_ // 2) & (s_ < t_))
    win = np.repeat(np.array([2, 4, 8, 16], np.float32), 64).reshape(2, P).T
    cnt0 = 1.0 / np.minimum(j[None, None] + 1, win[:, :, None])
    rk = np.zeros((P, RB, 2), np.float32)
    r_k = i["r_k"][0].reshape(RB, 2, HD)
    rk[:HD, :, 0], rk[HD:, :, 1] = r_k[:, 0].T, r_k[:, 1].T
    pm = np.zeros((P, 2, P), np.float32)
    for g in range(4):
        pm[64 * (g % 2):64 * (g % 2) + 64, g // 2, 64 * (g % 2):64 * (g % 2) + 64] = i["pool_map"][0, g]
    c = lambda a: np.ascontiguousarray(a, dtype=np.float32)
    return {
        "xT": xt, "x": x, "gpreT": blocks(i["norm_mix_pre"][0]), "gffnT": blocks(i["norm_ffn_pre"][0]),
        "gpost": rows(i["norm_mix_post"][0]), "gffnpost": rows(i["norm_ffn_post"][0]),
        "muT": blocks(i["mu_shift"][0]),
        "stshiftT": np.ascontiguousarray(i["state_shift"][0].reshape(NSEQ, NSH, P).transpose(2, 1, 0)),
        "w_in": wblk(i["w_in"][0]), "w_ffn_in": wblk(wf), "w_ffn_out": i["w_ffn_out"][0],
        "w_branch": np.concatenate([i["w_branch_rwkv"][0], i["w_branch_pool"][0]]), "w_out": i["w_out"][0],
        "wdec": np.concatenate([i["w_decay_up"][0], i["decay_bias"][0][None]]), "wiclr": i["w_iclr_up"][0],
        "bicl": blocks(i["iclr_bias"][0]), "wgate": i["w_gate_up"][0], "kk": blocks(i["k_k"][0]),
        "ka": blocks(i["k_a"][0]), "rk": rk, "lnw": rows(i["ln_x_w"][0]), "lnb": rows(i["ln_x_b"][0]),
        "pmap": pm, "pscale": blocks(i["pool_scale"][0]),
        "s0": np.ascontiguousarray(i["state_wkv"][0].reshape(NSEQ, RB, 2, HD, HD).transpose(2, 4, 1, 0, 3).reshape(P, RB, NSEQ, HD)),
        "pool0": np.ascontiguousarray(i["state_pool"][0].reshape(NSEQ, HIST, 2, P).transpose(3, 2, 0, 1)),
        "trip": c(trip), "tris": c(tris),
        "maskp": np.stack([strict, incl, strict, incl], 1).astype(np.uint32),
        "masks": np.ascontiguousarray(np.stack([strict & same, incl & same] * 2, 1)[:TS, :, :TS]).astype(np.uint32),
        "lvl": c(np.stack(lv, 1)), "w1": c(w1),
        "ident": c(np.eye(P)), "hsel": c(j[:, None] // HD == np.arange(2)[None]),
        "cnt0": c(cnt0), "cnt1": c(np.broadcast_to(1.0 / win[:, :, None], (P, 2, P))),
        "sel": c(js[:, None] // LSEQ == np.arange(NSEQ)[None]),
    }


def kernel(**inputs):
    import concourse.bacc as bacc
    import numpy as np
    from concourse.bass_utils import run_bass_kernel_spmd

    arrays = lay_out({k: np.asarray(v) for k, v in inputs.items()})
    nc = bacc.Bacc("TRN2", target_bir_lowering=False, num_devices=1)
    build(nc, arrays)
    r = run_bass_kernel_spmd(nc, [{f"in_{n}": a for n, a in arrays.items()}], core_ids=[0]).results[0]
    y = np.asarray(r["o_y"])
    unshift = lambda a: a.transpose(*range(2, a.ndim), 1, 0).reshape(1, -1, NSH * P)
    wkvp = np.asarray(r["o_wkvp"]).reshape(2, HD, RB, HD).transpose(2, 0, 3, 1).reshape(1, 1, H, HD, HD)
    wkvs = np.asarray(r["o_wkvs"]).reshape(2, HD, RB, NSEQ, HD).transpose(3, 2, 0, 4, 1).reshape(1, NSEQ, H, HD, HD)
    poolp = np.asarray(r["o_poolp"]).transpose(2, 1, 0).reshape(1, 1, HIST, 2 * P)
    pools = np.asarray(r["o_pools"]).transpose(2, 3, 1, 0).reshape(1, NSEQ, HIST, 2 * P)
    return (y[:TP].reshape(1, TP, D), y[TP:].reshape(NSEQ, LSEQ, D), wkvp, unshift(np.asarray(r["o_shp"])), poolp,
            wkvs, unshift(np.asarray(r["o_shs"])), pools)
```
